# Optimizing a Trainium2 kernel written in Bass

```python
import math
import jax, jax.numpy as jnp
from jax import lax
import numpy as np

D_MODEL = 1024
BATCH = 1
SEQ = 256
DEPTH = 1

RMS_EPS = 1e-6
NEG_BIG = -1e30
TINY = 1e-20
HG_HEADS = 4
HG_DK = 128
HG_DV = 128
HG_CHUNK = 64
MOBA_HEADS = 4
MOBA_DH = 128
MOBA_BLOCK = 256
MOBA_TOPK = 3
MOBA_Q_CHUNK = 32
DSA_HEADS = 4
DSA_DH = 128
DSA_KV_RANK = 256
IDX_HEADS = 8
IDX_DIM = 64
DSA_TOPK_MAX = 256
DSA_Q_BLOCK = 128
REL_BUCKETS = 32
REL_MAX_DIST = 2048
N_BRANCH = 3
D_FF = ((8 * D_MODEL // 3 + 255) // 256) * 256
HG_W = HG_HEADS * HG_DV
MOBA_W = MOBA_HEADS * MOBA_DH
DSA_W = DSA_HEADS * DSA_DH
IN_SIZES = (HG_HEADS * HG_DK, HG_HEADS * HG_DK, HG_W, HG_W,
            MOBA_W, MOBA_W, MOBA_W,
            DSA_W, DSA_KV_RANK,
            IDX_HEADS * IDX_DIM, IDX_DIM, IDX_HEADS,
            N_BRANCH * D_MODEL)
IN_WIDTH = sum(IN_SIZES)

kernel_name = 'hybrid_hgrn2_moba_dsa_gated_block'

def rms_norm(x, w):
    xf = x.astype(jnp.float32)
    y = xf * lax.rsqrt(jnp.mean(xf * xf, axis=-1, keepdims=True) + RMS_EPS)
    return (y * w.astype(jnp.float32)).astype(x.dtype)

def layer_norm(x, w, b):
    xf = x.astype(jnp.float32)
    mu = jnp.mean(xf, axis=-1, keepdims=True)
    xc = xf - mu
    y = xc * lax.rsqrt(jnp.mean(xc * xc, axis=-1, keepdims=True) + RMS_EPS)
    return (y * w.astype(jnp.float32) + b.astype(jnp.float32)).astype(x.dtype)

def rel_bucket(dist):
    n = jnp.maximum(dist, 0)
    exact = REL_BUCKETS // 2
    nf = jnp.maximum(n, exact).astype(jnp.float32)
    large = exact + (jnp.log(nf / exact) / math.log(REL_MAX_DIST / exact) * (REL_BUCKETS - exact)).astype(jnp.int32)
    large = jnp.minimum(large, REL_BUCKETS - 1)
    return jnp.where(n < exact, n, large)

def chunk_gated_recurrence(q, k, log_f, v):
    B, S, H, DK = q.shape
    DV = v.shape[-1]
    nc = S // HG_CHUNK

    def chunks(a):
        return a.reshape(B, nc, HG_CHUNK, H, a.shape[-1]).transpose(1, 0, 3, 2, 4)

    causal = jnp.tril(jnp.ones((HG_CHUNK, HG_CHUNK), dtype=bool))

    def step(state, inp):
        qc, kc, gc, vc = inp
        b = jnp.cumsum(gc, axis=2)
        o_inter = jnp.einsum('bhcd,bhde->bhce', qc * jnp.exp(b), state)
        diff = b[:, :, :, None, :] - b[:, :, None, :, :]
        decay = jnp.exp(jnp.where(causal[:, :, None], diff, NEG_BIG))
        scores = jnp.einsum('bhid,bhijd,bhjd->bhij', qc, decay, kc)
        o = o_inter + jnp.einsum('bhij,bhje->bhie', scores, vc)
        b_last = b[:, :, -1:, :]
        state = (jnp.exp(b_last[:, :, 0, :])[..., None] * state
                 + jnp.einsum('bhjd,bhje->bhde', kc * jnp.exp(b_last - b), vc))
        return state, o

    s0 = jnp.zeros((B, H, DK, DV), jnp.float32)
    _, o = lax.scan(step, s0, (chunks(q), chunks(k), chunks(log_f), chunks(v)))
    return o.transpose(1, 0, 3, 2, 4).reshape(B, S, H, DV)

def hgrn2_mixer(q, f_pre, i, g, lb, norm_w):
    B, S, _ = q.shape
    f32 = jnp.float32
    qf = q.reshape(B, S, HG_HEADS, HG_DK).astype(f32)
    fp = f_pre.reshape(B, S, HG_HEADS, HG_DK).astype(f32)
    v = i.reshape(B, S, HG_HEADS, HG_DV).astype(f32)
    lbh = lb.reshape(HG_HEADS, HG_DK).astype(f32)
    f = lbh + (1.0 - lbh) * jax.nn.sigmoid(fp)
    log_f = jnp.log(jnp.maximum(f, TINY))
    k = (1.0 - lbh) * jax.nn.sigmoid(-fp)
    o = chunk_gated_recurrence(qf, k, log_f, v)
    gate = jax.nn.silu(g.reshape(B, S, HG_HEADS, HG_DV).astype(f32))
    o = rms_norm(o, norm_w) * gate
    return o.reshape(B, S, HG_W).astype(q.dtype)

def moba_attention(q, k, v, rel_table):
    B, S, H, DH = q.shape
    f32 = jnp.float32
    nb = -(-S // MOBA_BLOCK)
    pad = nb * MOBA_BLOCK - S
    kp = jnp.pad(k, ((0, 0), (0, pad), (0, 0), (0, 0)))
    vp = jnp.pad(v, ((0, 0), (0, pad), (0, 0), (0, 0)))
    kb = kp.reshape(B, nb, MOBA_BLOCK, H, DH).transpose(0, 3, 1, 2, 4)
    vb = vp.reshape(B, nb, MOBA_BLOCK, H, DH).transpose(0, 3, 1, 2, 4)
    k_mean = jnp.mean(kb.astype(f32), axis=3).astype(q.dtype)
    n_sel = min(MOBA_TOPK, nb - 1)
    scale = DH ** -0.5
    nq = S // MOBA_Q_CHUNK
    q_chunks = q.reshape(B, nq, MOBA_Q_CHUNK, H, DH).transpose(1, 0, 2, 3, 4)
    starts = jnp.arange(nq, dtype=jnp.int32) * MOBA_Q_CHUNK
    b_ix = jnp.arange(B)[:, None, None, None]
    h_ix = jnp.arange(H)[None, None, :, None]
    h_ix5 = jnp.arange(H)[None, None, :, None, None]
    offs = jnp.arange(MOBA_BLOCK, dtype=jnp.int32)
    blk_ids = jnp.arange(nb, dtype=jnp.int32)

    def one_chunk(args):
        qc, start = args
        t = start + jnp.arange(MOBA_Q_CHUNK, dtype=jnp.int32)
        blk = start // MOBA_BLOCK
        k_own = lax.dynamic_slice_in_dim(kp, blk * MOBA_BLOCK, MOBA_BLOCK, axis=1)
        v_own = lax.dynamic_slice_in_dim(vp, blk * MOBA_BLOCK, MOBA_BLOCK, axis=1)
        dist_own = t[:, None] - (blk * MOBA_BLOCK + offs)[None, :]
        l_own = jnp.einsum('bqhd,bkhd->bqhk', qc, k_own).astype(f32) * scale
        l_own = l_own + rel_table[rel_bucket(dist_own)].astype(f32).transpose(0, 2, 1)
        l_own = jnp.where((dist_own >= 0)[:, None, :], l_own, NEG_BIG)
        if n_sel == 0:
            p = jax.nn.softmax(l_own, axis=-1).astype(v.dtype)
            return jnp.einsum('bqhk,bkhd->bqhd', p, v_own)
        gate = jnp.einsum('bqhd,bhnd->bqhn', qc, k_mean).astype(f32)
        gate = jnp.where(blk_ids < blk, gate, NEG_BIG)
        _, sel = lax.top_k(gate, n_sel)
        k_sel = kb[b_ix, h_ix, sel]
        v_sel = vb[b_ix, h_ix, sel]
        dist_sel = t[None, :, None, None, None] - (sel[..., None] * MOBA_BLOCK + offs)
        l_sel = jnp.einsum('bqhd,bqhknd->bqhkn', qc, k_sel).astype(f32) * scale
        l_sel = l_sel + rel_table[rel_bucket(dist_sel), h_ix5].astype(f32)
        l_sel = jnp.where((sel < blk)[..., None], l_sel, NEG_BIG)
        logits = jnp.concatenate([l_sel.reshape(B, MOBA_Q_CHUNK, H, n_sel * MOBA_BLOCK), l_own], axis=-1)
        p = jax.nn.softmax(logits, axis=-1).astype(v.dtype)
        p_sel = p[..., :n_sel * MOBA_BLOCK].reshape(B, MOBA_Q_CHUNK, H, n_sel, MOBA_BLOCK)
        p_own = p[..., n_sel * MOBA_BLOCK:]
        return (jnp.einsum('bqhkn,bqhknd->bqhd', p_sel, v_sel)
                + jnp.einsum('bqhk,bkhd->bqhd', p_own, v_own))

    out = lax.map(one_chunk, (q_chunks, starts))
    return out.transpose(1, 0, 2, 3, 4).reshape(B, S, H * DH)

def dsa_attention(q, c_kv, w_uk, w_uv, iq, ik, iw, rel_table, n_keep):
    B, S, H, DH = q.shape
    f32 = jnp.float32
    q_abs = jnp.einsum('bshd,rhd->bshr', q, w_uk)
    nblk = S // DSA_Q_BLOCK

    def blocks(a):
        return a.reshape((B, nblk, DSA_Q_BLOCK) + a.shape[2:]).swapaxes(0, 1)

    starts = jnp.arange(nblk, dtype=jnp.int32) * DSA_Q_BLOCK
    key_pos = jnp.arange(S, dtype=jnp.int32)
    scale = DH ** -0.5

    def one_block(args):
        qa, iqb, iwb, start = args
        t = start + jnp.arange(DSA_Q_BLOCK, dtype=jnp.int32)
        s_idx = jnp.einsum('bqhe,bse->bqhs', iqb, ik).astype(f32) * (IDX_DIM ** -0.5)
        score = jnp.einsum('bqh,bqhs->bqs', iwb.astype(f32), jax.nn.relu(s_idx))
        score = jnp.where(key_pos[None, :] <= t[:, None], score, NEG_BIG)
        _, idx = lax.top_k(score, n_keep)
        c_sel = jax.vmap(lambda cb, ib: cb[ib])(c_kv, idx)
        dist = t[None, :, None] - idx
        logits = jnp.einsum('bqhr,bqkr->bqhk', qa, c_sel).astype(f32) * scale
        logits = logits + rel_table[rel_bucket(dist)].astype(f32).transpose(0, 1, 3, 2)
        logits = jnp.where((dist >= 0)[:, :, None, :], logits, NEG_BIG)
        p = jax.nn.softmax(logits, axis=-1).astype(c_kv.dtype)
        return jnp.einsum('bqhk,bqkr->bqhr', p, c_sel)

    o_lat = lax.map(one_block, (blocks(q_abs), blocks(iq), blocks(iw), starts))
    o_lat = o_lat.swapaxes(0, 1).reshape(B, S, H, DSA_KV_RANK)
    return jnp.einsum('bshr,rhd->bshd', o_lat, w_uv).reshape(B, S, H * DH)

def setup_inputs(seed: int = 0) -> dict:
    key = jax.random.key(seed)
    ks = jax.random.split(key, 24)
    f32 = jnp.float32

    def nrm(k, shape, scale):
        return jax.random.normal(k, shape, f32) * scale

    def gain(k, shape):
        return 1.0 + 0.05 * jax.random.normal(k, shape, f32)

    return {
        'x': nrm(ks[0], (BATCH, SEQ, D_MODEL), 1.0),
        'w_in': nrm(ks[1], (DEPTH, D_MODEL, IN_WIDTH), D_MODEL ** -0.5),
        'pre_mix_norm': gain(ks[2], (DEPTH, D_MODEL)),
        'post_mix_norm': gain(ks[3], (DEPTH, D_MODEL)),
        'pre_ffn_norm': gain(ks[4], (DEPTH, D_MODEL)),
        'post_ffn_norm': gain(ks[5], (DEPTH, D_MODEL)),
        'hg_lb_logits': nrm(ks[6], (DEPTH, HG_HEADS * HG_DK), 0.5),
        'hg_norm_w': gain(ks[7], (DEPTH, HG_DV)),
        'dsa_kv_norm': gain(ks[8], (DEPTH, DSA_KV_RANK)),
        'dsa_w_uk': nrm(ks[9], (DEPTH, DSA_KV_RANK, DSA_HEADS, DSA_DH), DSA_KV_RANK ** -0.5),
        'dsa_w_uv': nrm(ks[10], (DEPTH, DSA_KV_RANK, DSA_HEADS, DSA_DH), DSA_KV_RANK ** -0.5),
        'idx_k_norm_w': gain(ks[11], (DEPTH, IDX_DIM)),
        'idx_k_norm_b': nrm(ks[12], (DEPTH, IDX_DIM), 0.02),
        'rel_bias': nrm(ks[13], (REL_BUCKETS, MOBA_HEADS + DSA_HEADS), 0.5),
        'w_branch_a': nrm(ks[14], (DEPTH, HG_W, D_MODEL), HG_W ** -0.5),
        'w_branch_b': nrm(ks[15], (DEPTH, MOBA_W, D_MODEL), MOBA_W ** -0.5),
        'w_branch_c': nrm(ks[16], (DEPTH, DSA_W, D_MODEL), DSA_W ** -0.5),
        'w_out': nrm(ks[17], (DEPTH, D_MODEL, D_MODEL), D_MODEL ** -0.5),
        'w_ffn_in': nrm(ks[18], (DEPTH, D_MODEL, 2 * D_FF), D_MODEL ** -0.5),
        'w_ffn_out': nrm(ks[19], (DEPTH, D_FF, D_MODEL), D_FF ** -0.5),
    }

def reference(x, w_in, pre_mix_norm, post_mix_norm, pre_ffn_norm, post_ffn_norm,
              hg_lb_logits, hg_norm_w, dsa_kv_norm, dsa_w_uk, dsa_w_uv,
              idx_k_norm_w, idx_k_norm_b, rel_bias, w_branch_a, w_branch_b, w_branch_c,
              w_out, w_ffn_in, w_ffn_out):
    f32 = jnp.float32
    B, S, _ = x.shape
    lbp = jax.nn.softmax(hg_lb_logits.astype(f32), axis=0)
    lower_bounds = jnp.cumsum(lbp, axis=0) - lbp[0]
    bias_b = rel_bias[:, :MOBA_HEADS]
    bias_c = rel_bias[:, MOBA_HEADS:]
    n_keep = min(DSA_TOPK_MAX, S // 4)
    splits = [int(s) for s in np.cumsum(IN_SIZES)[:-1]]
    for l in range(DEPTH):
        h = rms_norm(x, pre_mix_norm[l])
        proj = h @ w_in[l]
        (hq, hf, hi, hg, mq, mk, mv, dq, dkv, iq, ik, iw, gates) = jnp.split(proj, splits, axis=-1)
        y_a = hgrn2_mixer(hq, hf, hi, hg, lower_bounds[l], hg_norm_w[l])
        y_b = moba_attention(mq.reshape(B, S, MOBA_HEADS, MOBA_DH),
                             mk.reshape(B, S, MOBA_HEADS, MOBA_DH),
                             mv.reshape(B, S, MOBA_HEADS, MOBA_DH), bias_b)
        c_kv = rms_norm(dkv, dsa_kv_norm[l])
        ik_n = layer_norm(ik, idx_k_norm_w[l], idx_k_norm_b[l])
        y_c = dsa_attention(dq.reshape(B, S, DSA_HEADS, DSA_DH), c_kv, dsa_w_uk[l], dsa_w_uv[l],
                            iq.reshape(B, S, IDX_HEADS, IDX_DIM), ik_n, iw * (IDX_HEADS ** -0.5),
                            bias_c, n_keep)
        g = jax.nn.sigmoid(gates.reshape(B, S, N_BRANCH, D_MODEL))
        merged = (g[:, :, 0] * (y_a @ w_branch_a[l])
                  + g[:, :, 1] * (y_b @ w_branch_b[l])
                  + g[:, :, 2] * (y_c @ w_branch_c[l]))
        x = x + rms_norm(merged @ w_out[l], post_mix_norm[l])
        h2 = rms_norm(x, pre_ffn_norm[l])
        gate, up = jnp.split(h2 @ w_ffn_in[l], 2, axis=-1)
        x = x + rms_norm((jax.nn.silu(gate) * up) @ w_ffn_out[l], post_ffn_norm[l])
    return x


_drawn_inputs = setup_inputs


def setup_inputs(seed=0):
    import zlib

    import numpy as np

    out = dict(_drawn_inputs(seed))
    spreads = {}
    factors = {'dsa_kv_norm': 2.813, 'hg_norm_w': 3.543}
    for name, (base, spread) in spreads.items():
        noise = np.random.default_rng([zlib.crc32(name.encode()), seed]).standard_normal(out[name].shape)
        drawn = base * np.exp(spread * noise) if base else spread * noise
        out[name] = __import__('jax').numpy.asarray(drawn.astype(out[name].dtype))
    for name, factor in factors.items():
        out[name] = (out[name] * factor).astype(out[name].dtype)
    return out
```

```python
from contextlib import ExitStack

import concourse.bass as bass
import numpy as np
from concourse import mybir

F32 = mybir.dt.float32
F32R = mybir.dt.float32r
U8 = mybir.dt.uint8
ALU = mybir.AluOpType
ACT = mybir.ActivationFunctionType
AX = mybir.AxisListType

P = 128
D = 1024
S = 256
TT = S // P
KT = D // P
H = 4
HW = H * P
NI, DI = 8, 64
RK = 256
RT = RK // P
DFF = 2816
FT = DFF // P
NKEEP = 64
EPS, NEG, TINY = 1e-6, -1e30, 1e-20
TAKEN = -3e38
SCALE = float(P) ** -0.5
BUCKETS, TW = 32, 384

C_HQ, C_HF, C_HI, C_HG, C_MQ, C_MK, C_MV, C_DQ, C_CKV, C_IW_END, C_G = (
    0, 512, 1024, 1536, 2048, 2560, 3072, 3584, 4096, 4936, 4936)

IN_BLOCKS = [("lat", C_CKV, 512), ("idx", C_CKV + 512, C_IW_END - C_CKV - 512), ("dq", C_DQ, 512),
             ("hf", C_HF, 512), ("hq", C_HQ, 512), ("hi", C_HI, 512), ("mq", C_MQ, 512), ("mk", C_MK, 512),
             ("mv", C_MV, 512), ("hg", C_HG, 512)]
BRANCHES = (1, 2, 0)


def plan_blocks():
    blocks = [(n, KT, w) for n, _, w in IN_BLOCKS]
    for c in range(2):
        blocks += [(f"gate{b}{c}", KT, 512) for b in BRANCHES]
        blocks += [(f"branch{b}{c}", H, 512) for b in BRANCHES]
    blocks += [(f"out{c}", KT, 512) for c in range(2)]
    for j in range(DFF // 512):
        blocks += [(f"fg{j}", KT, 512), (f"fu{j}", KT, 512)]
    blocks += [("fgu", KT, 512)]
    blocks += [(f"down{c}", FT, 512) for c in range(2)]
    return blocks


BLOCKS = plan_blocks()
UNITS = [(b, kt, w) for b, (_, n, w) in enumerate(BLOCKS) for kt in range(0, n, 2)]
OFFSETS = [int(v) for v in np.cumsum([0] + [P * 2 * w for _, _, w in UNITS])]
BLOCK = {n: b for b, (n, _, _) in enumerate(BLOCKS)}
LAST_UNIT = {BLOCKS[b][0]: u for u, (b, _, _) in enumerate(UNITS)}
FIRST_UNIT = {BLOCKS[b][0]: u for u, (b, _, _) in reversed(list(enumerate(UNITS)))}

NOT_LAST = list(int(v) for v in np.cumsum([kt + 2 != BLOCKS[b][1] for b, kt, _ in UNITS]))

RAW, SPLIT = 3, 5

LEVELS = [1, 2, 4, 8, 16, 32, 64]
JOBS = (["hT0", "hT1", "hT2", "hT3", "rel", "ckvT", "iqT0", "iqT1", "ikT", "kc0", "kc1", "vc0", "vc1"]
        + [f"ix{i}" for i in range(6)] + ["dqT0", "dqT1", "hfT0", "hfT1", "dl0", "dl1", "dl2", "hqT0", "hqT1",
                                          "diag0", "diag1", "L1_0", "L1_1", "dP0", "dP1", "dP2", "L2_0", "L2_1",
                                          "dO0", "dO1", "L4_0", "L4_1", "mqT0", "mqT1", "L8_0", "L8_1", "L16_0", "L16_1",
                                          "mkT0", "mkT1", "L32_0", "L32_1", "ml0", "ml1", "ml2", "L64_0", "L64_1", "L128",
                                          "mP0", "mP1", "mP2", "ho0", "ho1", "mO0", "mO1", "yaT0", "yaT1",
                                          "mT0", "mT1", "mT2", "mT3", "h2T0", "h2T1", "h2T2", "h2T3"]
        + [f"fT{i}" for i in range(FT // 2)])
JOB = {n: m for m, n in enumerate(JOBS)}
INDEXER = [(0, (0, 2, 4, 6)), (0, (1, 3, 5, 7)), (1, (0, 2)), (1, (4, 6)), (1, (1, 3)), (1, (5, 7))]


def bias_runs():
    n = np.arange(S)
    half = BUCKETS // 2
    nf = np.maximum(n, half).astype(np.float32)
    large = half + (np.log(nf / half) / np.log(2048 / half) * (BUCKETS - half)).astype(np.int32)
    return np.where(n < half, n, np.minimum(large, BUCKETS - 1))


def constants():
    eye = np.eye(P, dtype=np.float32)
    i, j = np.arange(P)[None, :], np.arange(P)[:, None]
    levels = np.stack([((i // (2 * s)) == (j // (2 * s))) & ((i // s) % 2 == 1) & ((j // s) % 2 == 0)
                       for s in LEVELS], 1).astype(np.float32)
    hot = np.zeros((BUCKETS + 1, TW), np.float32)
    bucket = bias_runs()
    for m in range(TW):
        dist = S - 1 - m
        hot[bucket[dist] if dist >= 0 else BUCKETS, m] = 1.0
    return eye, np.ascontiguousarray(levels.reshape(P, -1)), hot


COLS = {"pre_mix": (0, 8), "pre_ffn": (8, 16), "lb": (16, 20), "kv_norm": (20, 22), "ik_w": (22, 23), "ik_b": (23, 24)}
NCOLS = 24


def build_block(nc, w_stream, x_in, cols_in, eye_in, levels_in, hot_in, rel_in, w_uk, w_uv,
                hg_norm, post_mix, post_ffn, out):
    ctx = ExitStack()
    with ctx:
        def sb(name, shape, dt=F32, stack=ctx):
            return stack.enter_context(nc.sbuf_tensor(name, shape, dt))

        def sem(name):
            return ctx.enter_context(nc.semaphore(name))

        raw = sb("raw", [P, RAW, 1024])
        wh = sb("wh", [P, SPLIT, 1024], F32R)
        wl = sb("wl", [P, SPLIT, 1024], F32R)
        hTh = sb("hTh", [P, KT, S], F32R)
        hTl = sb("hTl", [P, KT, S], F32R)
        eye = sb("eye", [P, P])
        cols = sb("cols", [P, NCOLS])
        st = sb("st", [P, 160])
        post = sb("post", [P, D])
        tmp = sb("tmp", [P, 2, 512])
        sig = sb("sig", [P, 3, TT, 512])
        yh = [sb(f"yh{b}", [P, H, S], F32R) for b in range(3)]
        yl = [sb(f"yl{b}", [P, H, S], F32R) for b in range(3)]

        early = ExitStack()
        x0 = sb("x0", [P, TT, D], stack=early)
        stage = sb("stage", [P, 3, TT, 512], stack=early)
        ikn = sb("ikn", [P, TT, P], stack=early)
        ikc = sb("ikc", [P, TT, DI], stack=early)
        iws = sb("iws", [P, TT, NI], stack=early)
        ckvT = sb("ckvT", [P, RT, S], stack=early)
        ikT = sb("ikT", [P, S], stack=early)
        wuk = sb("wuk", [P, RT, HW], stack=early)
        wuv = sb("wuv", [P, RT, HW], stack=early)
        hqT = sb("hqT", [P, H, S], stack=early)
        iqT = hqT
        kT = sb("kT", [P, H, S], stack=early)
        pre = sb("pre", [P, H, S], stack=early)
        suf = sb("suf", [P, H, S], stack=early)
        att = [w[:].rearrange("p r n -> p (r n)").rearrange("p (h t) -> p h t", h=H) for w in (wuk, wuv)]
        tri = sb("tri", [P, H, TW], stack=early)
        qT = sb("qT", [P, H, S], stack=early)
        kcT = sb("kcT", [P, H, S], stack=early)
        vc = sb("vc", [P, TT, HW], stack=early)
        mv = sb("mv", [P, TT, HW], stack=early)
        hv = x0[:, 0].rearrange("p (t n) -> p t n", t=TT)
        gw = x0[:, 1].rearrange("p (t n) -> p t n", t=TT)
        bias = sb("bias", [P, 2 * H, S], stack=early)
        prob = sb("prob", [P, H * TW], stack=early)
        probT = sb("probT", [P, H * TW], stack=early)
        rel = sb("rel", [BUCKETS + 1, 2 * H], stack=early)
        relu = tmp
        score = sb("score", [P, TW], stack=early)
        work = sb("work", [P, TW], stack=early)
        rel8 = score[0:2 * H]
        hot = work[0:BUCKETS + 1]
        top8 = sb("top8", [P, 2, 8], stack=early)
        lvl = sb("lvl", [P, len(LEVELS) * P], U8, stack=early)
        hgn = sb("hgn", [P, P], stack=early)
        early.close()
        late = ExitStack()
        mTh = sb("mTh", [P, KT, S], F32R, stack=late)
        mTl = sb("mTl", [P, KT, S], F32R, stack=late)
        merged = sb("merged", [P, TT, D], stack=late)
        x1 = sb("x1", [P, TT, D], stack=late)
        mo = sb("mo", [P, TT, D], stack=late)
        fT_h = sb("fTh", [P, FT, S], F32R, stack=late)
        fT_l = sb("fTl", [P, FT, S], F32R, stack=late)
        fg = sb("fg", [P, 2, TT, 512], stack=late)
        fa = sb("fa", [P, 2, TT, 512], stack=late)
        late.close()

        bank = [ctx.enter_context(nc.psum_tensor(f"bank{b}", [P, 512], F32)) for b in range(8)]
        scratch = nc.dram_tensor("bias_scratch", [2 * H * P * TW], F32, kind="Internal").ap()

        raw_loaded = [sem(f"raw_loaded{i}") for i in range(RAW)]
        high_done, low_done, unit_used = sem("high_done"), sem("low_done"), sem("unit_used")
        bank_full = [sem(f"bank_full{b}") for b in range(8)]
        bank_read = [sem(f"bank_read{b}") for b in range(8)]
        x_loaded, eye_loaded, cols_loaded = sem("x_loaded"), sem("eye_loaded"), sem("cols_loaded")
        rel_loaded, lat_loaded, post_loaded, hgn_loaded = (
            sem("rel_loaded"), sem("lat_loaded"), sem("post_loaded"), sem("hgn_loaded"))
        x1_loaded, lvl_loaded = sem("x1_loaded"), sem("lvl_loaded")
        rel_row, rel_stored, bias_loaded = sem("rel_row"), sem("rel_stored"), sem("bias_loaded")
        act_step, dve_step, pool_step = sem("act_step"), sem("dve_step"), sem("pool_step")
        names = """ckv_ready down_rstd down_squares down_sums exp_done fT_high final_ready gates_ready h2_high h2_ready h2_rstd hT_high hT_ready hg_sig ik_ready ik_rstd ik_squares lat_rstd lat_squares lb_delta level_built logits_max mT_high merged o_rstd o_squares o_sums one_exp out_rstd out_squares out_sums prob_ready relu_used score_ready silu_last stored x1_ready x1_squares x_rstd x_squares y_high""".split()
        s = {n: sem(n) for n in names}

        def block_bank(name, t):
            n = BLOCK[name]
            return 2 * (n % 2) + t, n // 2

        def job_bank(name):
            m = JOB[name]
            return 4 + m % 4, m // 4

        def wait_block(eng, name, t):
            b, n = block_bank(name, t)
            eng.wait_ge(bank_full[b], n + 1)
            return bank[b]

        def wait_job(eng, name):
            b, n = job_bank(name)
            eng.wait_ge(bank_full[b], n + 1)
            return bank[b]

        def block_read(name, t):
            b, n = block_bank(name, t)
            return bank_read[b], n + 1

        def job_read(name):
            b, n = job_bank(name)
            return bank_read[b], n + 1

        def after_job(eng, name):
            eng.wait_ge(*job_read(name))

        def after_block(eng, name):
            eng.wait_ge(*block_read(name, TT - 1))

        def wait_unit_used(eng, u):
            b, kt, _ = UNITS[u]
            name, n_kt, _ = BLOCKS[b]
            if kt + 2 == n_kt:
                wait_block(eng, name, TT - 1)
            else:
                eng.wait_ge(unit_used, NOT_LAST[u])

        X_SS, X_RS, LAT_SS, LAT_RS, IK_MEAN, IK_SS, IK_RS = 0, 2, 4, 6, 8, 10, 12
        LB, OML, ONE = 16, 20, 24
        NMAX, SUM, RCP = 28, 44, 60
        O_SS, O_RS = 76, 84
        OUT_P, OUT_SS, OUT_RS, X1_SS, X1_RS = 92, 96, 98, 100, 102
        DN_P, DN_SS, DN_RS = 104, 108, 110
        HALF, RMS_TMP, ZERO = 112, 120, 130

        def col(name, i=0):
            a = COLS[name][0] + i
            return cols[:, a:a + 1]

        def stat(i, n=1):
            return st[:, i:i + n]

        tri3 = tri[:]
        prob3 = prob[:].rearrange("p (h k) -> p h k", h=H)
        probT3 = probT[:].rearrange("p (h k) -> p h k", h=H)
        lvl3 = lvl[:].rearrange("p (l k) -> p l k", l=len(LEVELS))

        def heads(ap, n=H):
            return ap.rearrange("p (h k) -> p h k", h=n)

        block = ctx.enter_context(nc.Block())

        @block.sync
        def _(sp):
            x_rows = x_in.rearrange("o (t p) d -> p (o t) d", p=P)
            for t in range(TT):
                sp.dma_start(x0[:, t], x_rows[:, t]).then_inc(x_loaded, 16)
            for u, (b, kt, w) in enumerate(UNITS):
                if u >= RAW:
                    sp.wait_ge(low_done, u - RAW + 1)
                src = w_stream[OFFSETS[u]:OFFSETS[u + 1]].rearrange("(p n) -> p n", p=P)
                sp.dma_start(raw[:, u % RAW, 0:2 * w], src).then_inc(raw_loaded[u % RAW], 16)
                if u == 8:
                    after_job(sp, "rel")
                    rows = rel8.rearrange("h (o m) -> h o m", o=1).to_broadcast([2 * H, P, TW])
                    sp.dma_start(scratch.rearrange("(h p m) -> h p m", h=2 * H, p=P), rows).then_inc(rel_stored, 16)
                if u == 12:
                    sp.wait_ge(rel_stored, 16)
                    skewed = bass.AP(scratch.tensor, P - 1, [[TW - 1, P], [P * TW, 2 * H], [1, S]])
                    sp.dma_start(bias[:], skewed).then_inc(bias_loaded, 16)
                if u == LAST_UNIT["branch01"]:
                    sp.wait_ge(s["merged"], 4)
                    sp.dma_start(x1[:], x_rows).then_inc(x1_loaded, 16)
                if u == LAST_UNIT["down0"]:
                    sp.wait_ge(s["x1_ready"], 4)
                    sp.dma_start(post[:], post_ffn.to_broadcast([P, D])).then_inc(post_loaded, 16)
            y_rows = out.rearrange("o (t p) d -> p (o t) d", p=P)
            for t in range(TT):
                sp.wait_ge(s["final_ready"], t + 1)
                sp.dma_start(y_rows[:, t], mo[:, t]).then_inc(s["stored"], 16)
            sp.wait_ge(s["stored"], 16 * TT)

        @block.scalar
        def _(act):
            last = [None]
            n_steps = [0]
            next_unit = [0]

            def did(ins, semaphore=None, value=None):
                if semaphore is None:
                    n_steps[0] += 1
                    semaphore, value = act_step, n_steps[0]
                ins.then_inc(semaphore, 1)
                last[0] = (semaphore, value)

            def settle():
                act.wait_ge(*last[0])

            def high_until(u_end):
                while next_unit[0] <= min(u_end, len(UNITS) - 1):
                    u = next_unit[0]
                    w = UNITS[u][2]
                    act.wait_ge(raw_loaded[u % RAW], 16 * (u // RAW + 1))
                    if u >= SPLIT:
                        wait_unit_used(act, u - SPLIT)
                    did(act.activation(wh[:, u % SPLIT, 0:2 * w], raw[:, u % RAW, 0:2 * w], ACT.Copy), high_done, u + 1)
                    next_unit[0] += 1

            act.dma_start(eye[:], eye_in).then_inc(eye_loaded, 16)
            act.dma_start(cols[:], cols_in).then_inc(cols_loaded, 16)
            act.dma_start(hot, hot_in).then_inc(rel_loaded, 16)
            act.dma_start(rel[0:BUCKETS, :], rel_in).then_inc(rel_loaded, 16)
            act.dma_start(wuk[:], w_uk.rearrange("(r p) n -> p r n", p=P)).then_inc(lat_loaded, 16)
            act.dma_start(wuv[:], w_uv.rearrange("(r p) n -> p r n", p=P)).then_inc(lat_loaded, 16)
            act.dma_start(prob[:, 0:len(LEVELS) * P], levels_in).then_inc(lvl_loaded, 16)
            act.dma_start(hgn[:], hg_norm.to_broadcast([P, P])).then_inc(hgn_loaded, 16)
            act.dma_start(post[:], post_mix.to_broadcast([P, D])).then_inc(post_loaded, 16)

            act.wait_ge(s["lb_delta"], 1)
            did(act.activation(stat(ONE, H), stat(ONE, H), ACT.Exp), s["one_exp"], 1)
            for j in range(4):
                after_job(act, f"hT{j}")
                did(act.activation(hTh[:, 2 * j:2 * j + 2, :].rearrange("p k t -> p (k t)"), tmp[:, j % 2], ACT.Copy),
                    s["hT_high"], j + 1)
                high_until(j)
            act.wait_ge(x_loaded, 32)
            act.wait_ge(s["hT_ready"], 4)
            for t in range(TT):
                for c in range(2):
                    if t or c:
                        settle()
                    did(act.activation(relu[:, c], x0[:, t, c * 512:(c + 1) * 512], ACT.Square,
                                       accum_out=stat(OUT_P + 2 * t + c)), s["x_squares"], 2 * t + c + 1)
            high_until(7)

            def stage_copy(name, slot, w, src_units):
                high_until(src_units)
                act.wait_ge(s["x_rstd"], 1)
                for t in range(TT):
                    ps = wait_block(act, name, t)
                    did(act.activation(stage[:, slot, t, 0:w], ps[:, 0:w], ACT.Copy, scale=stat(X_RS + t)), *block_read(name, t))

            stage_copy("lat", 0, 512, LAST_UNIT["lat"] + 4)
            for t in range(TT):
                settle()
                did(act.activation(relu[:, 0, 0:RK], stage[:, 0, t, 0:RK], ACT.Square, accum_out=stat(LAT_SS + t)), s["lat_squares"], t + 1)
            stage_copy("idx", 1, 328, LAST_UNIT["idx"] + 4)

            def copy_jobs(jobs, dst):
                for i, name in enumerate(jobs):
                    ps = wait_job(act, name)
                    did(act.activation(dst(i), ps[:, 0:512], ACT.Copy), *job_read(name))

            def flat(ap, i):
                return ap[:, 2 * i:2 * i + 2, :].rearrange("p h t -> p (h t)")

            high_until(13)
            copy_jobs(["iqT0"], lambda i: flat(iqT, 0))
            high_until(14)
            copy_jobs(["iqT1"], lambda i: flat(iqT, 1))
            stage_copy("dq", 2, 512, 15)
            copy_jobs(["kc0", "kc1"], lambda i: flat(kcT, i))
            high_until(16)
            copy_jobs(["vc0", "vc1"], lambda i: vc[:, i, :])
            for i in range(6):
                high_until(17 + i // 2)
                ps = wait_job(act, f"ix{i}")
                if i >= 2:
                    act.wait_ge(s["relu_used"], i - 1)
                did(act.activation(relu[:, i % 2], ps[:, 0:512], ACT.Relu, scale=DI ** -0.5), *job_read(f"ix{i}"))
            stage_copy("hf", 0, 512, 19)
            high_until(20)
            copy_jobs(["dqT0", "dqT1"], lambda i: flat(qT, i))
            high_until(22)
            for i in range(2):
                ps = wait_job(act, f"hfT{i}")
                did(act.activation(flat(pre, i), ps[:, 0:512], ACT.Sigmoid))
                did(act.activation(flat(kT, i), ps[:, 0:512], ACT.Sigmoid, scale=-1.0), *job_read(f"hfT{i}"))
            wait_job(act, "ikT")
            stage_copy("hq", 1, 512, 23)
            high_until(26)
            copy_jobs(["hqT0", "hqT1"], lambda i: flat(hqT, i))

            def exps(k):
                act.wait_ge(s["logits_max"], k + 1)
                for t in range(TT):
                    for h in range(H):
                        i = 8 * k + t * H + h
                        row = prob3[:, h, 0:P] if t == 0 else prob3[:, h, P:TW]
                        ins = act.activation(row, row, ACT.Exp, bias=stat(NMAX + i), accum_out=stat(SUM + i))
                        if t == TT - 1 and h == H - 1:
                            did(ins, s["exp_done"], k + 1)
                        else:
                            did(ins)

            def probT_copy(jobs):
                for i, name in enumerate(jobs):
                    ps = wait_job(act, name)
                    did(act.activation(probT[:, 512 * i:512 * (i + 1)], ps[:, 0:512], ACT.Copy), *job_read(name))

            def y_high(jobs, b, k):
                for i, name in enumerate(jobs):
                    ps = wait_job(act, name)
                    did(act.activation(flat(yh[b], i), ps[:, 0:512], ACT.Copy), s["y_high"], 2 * k + i + 1)

            def tokens(name, dst, units):
                high_until(units)
                for t in range(TT):
                    ps = wait_block(act, name, t)
                    did(act.activation(dst[:, t, :], ps[:, 0:512], ACT.Copy, scale=stat(X_RS + t)), *block_read(name, t))

            exps(0)
            tokens("hi", hv, LAST_UNIT["hi"] + 4)
            high_until(29)
            probT_copy(["dP0", "dP1", "dP2"])
            stage_copy("mq", 2, 512, LAST_UNIT["mq"] + 4)
            y_high(["dO0", "dO1"], 2, 0)
            high_until(34)
            copy_jobs(["mqT0", "mqT1"], lambda i: flat(qT, i))
            stage_copy("mk", 0, 512, LAST_UNIT["mk"] + 4)
            high_until(38)
            copy_jobs(["mkT0", "mkT1"], lambda i: flat(kcT, i))
            tokens("mv", mv, LAST_UNIT["mv"] + 4)
            high_until(40)
            exps(1)
            high_until(43)
            for t in range(TT):
                ps = wait_block(act, "hg", t)
                did(act.activation(gw[:, t, :], ps[:, 0:512], ACT.Sigmoid, scale=stat(X_RS + t)), s["hg_sig"], t + 1)
            probT_copy(["mP0", "mP1", "mP2"])
            high_until(45)
            for t in range(TT):
                ps = wait_job(act, f"ho{t}")
                did(act.activation(relu[:, t], ps[:, 0:512], ACT.Square), s["o_squares"], t + 1)
            high_until(46)
            y_high(["mO0", "mO1"], 1, 1)

            def gates(i, c):
                b = BRANCHES[i]
                name = f"gate{b}{c}"
                high_until(LAST_UNIT[name] + 4)
                if c:
                    after_block(act, f"branch{b}0")
                for t in range(TT):
                    ps = wait_block(act, name, t)
                    did(act.activation(sig[:, b, t], ps[:, 0:512], ACT.Sigmoid, scale=stat(X_RS + t)), *block_read(name, t))

            gates(0, 0)
            gates(1, 0)
            y_high(["yaT0", "yaT1"], 0, 2)
            gates(2, 0)
            gates(0, 1)
            for j in range(2):
                ps = wait_job(act, f"mT{j}")
                did(act.activation(flat(mTh, j), ps[:, 0:512], ACT.Copy), s["mT_high"], j + 1)
            gates(1, 1)
            gates(2, 1)
            high_until(LAST_UNIT["branch01"] + 3)
            for j in range(2, 4):
                high_until(LAST_UNIT["branch01"] + 2 + j - 1)
                ps = wait_job(act, f"mT{j}")
                did(act.activation(flat(mTh, j), ps[:, 0:512], ACT.Copy), s["mT_high"], j + 1)
            for c in range(2):
                high_until(LAST_UNIT[f"out{c}"] + 4)
                for t in range(TT):
                    ps = wait_block(act, f"out{c}", t)
                    settle()
                    did(act.activation(tmp[:, c], ps[:, 0:512], ACT.Square, accum_out=stat(OUT_P + 2 * t + c)),
                        s["out_squares"], 2 * c + t + 1)
            high_until(LAST_UNIT["out1"] + 5)
            for j in range(4):
                after_job(act, f"h2T{j}")
                did(act.activation(hTh[:, 2 * j:2 * j + 2, :].rearrange("p k t -> p (k t)"), fa[:, 0, j % 2], ACT.Copy),
                    s["h2_high"], j + 1)
            for t in range(TT):
                settle()
                act.wait_ge(s["x1_ready"], 4)
                did(act.activation(mo[:, t, :], x1[:, t, :], ACT.Square, accum_out=stat(X1_SS + t)), s["x1_squares"], t + 1)

            def silu(name, j, w):
                act.wait_ge(s["h2_rstd"], 1)
                if j >= 2:
                    after_block(act, f"fu{j - 2}")
                for t in range(TT):
                    ps = wait_block(act, name, t)
                    ins = act.activation(fg[:, j % 2, t, 0:w], ps[:, 0:w], ACT.Silu, scale=stat(X1_RS + t))
                    if w == 512:
                        did(ins, *block_read(name, t))
                    else:
                        did(ins, s["silu_last"], t + 1)

            def f_high(j, n):
                for i in range(2 * j, 2 * j + n):
                    ps = wait_job(act, f"fT{i}")
                    did(act.activation(fT_h[:, 2 * i:2 * i + 2, :].rearrange("p k t -> p (k t)"), ps[:, 0:512], ACT.Copy),
                        s["fT_high"], i + 1)

            for j in range(5):
                if j:
                    high_until(LAST_UNIT[f"fu{j - 1}"] + 6)
                    f_high(j - 1, 2)
                high_until(LAST_UNIT[f"fg{j}"] + 4)
                silu(f"fg{j}", j, 512)
            high_until(LAST_UNIT["fu4"] + 6)
            f_high(4, 2)
            high_until(LAST_UNIT["fgu"] + 4)
            silu("fgu", 5, 256)
            high_until(LAST_UNIT["fgu"] + 7)
            f_high(5, 1)
            for c in range(2):
                high_until(LAST_UNIT[f"down{c}"] + 4)
                for t in range(TT):
                    ps = wait_block(act, f"down{c}", t)
                    settle()
                    did(act.activation(tmp[:, t], ps[:, 0:512], ACT.Square, accum_out=stat(DN_P + 2 * t + c)),
                        s["down_squares"], 2 * c + t + 1)

        @block.vector
        def _(dve):
            last = [None]
            n_steps = [0]
            next_unit = [0]

            def did(ins, semaphore=None, value=None):
                if semaphore is None:
                    n_steps[0] += 1
                    semaphore, value = dve_step, n_steps[0]
                ins.then_inc(semaphore, 1)
                last[0] = (semaphore, value)

            def settle():
                if last[0] is not None:
                    dve.wait_ge(*last[0])

            def low_until(u_end):
                while next_unit[0] <= min(u_end, len(UNITS) - 1):
                    u = next_unit[0]
                    w = UNITS[u][2]
                    dve.wait_ge(high_done, u + 1)
                    did(dve.tensor_tensor(wl[:, u % SPLIT, 0:2 * w], raw[:, u % RAW, 0:2 * w],
                                          wh[:, u % SPLIT, 0:2 * w].bitcast(F32), ALU.subtract), low_done, u + 1)
                    next_unit[0] += 1

            def flat(ap, i):
                return ap[:, 2 * i:2 * i + 2, :].rearrange("p h t -> p (h t)")

            def low_of_bank(ps, low, high, reads):
                did(dve.tensor_tensor(low, ps[:, 0:512], high.bitcast(F32), ALU.subtract), *reads)

            dve.wait_ge(cols_loaded, 16)
            a, b_ = COLS["lb"]
            did(dve.tensor_tensor(stat(ONE, H), cols[:, a:b_], cols[:, a:b_], ALU.subtract), s["lb_delta"], 1)

            for j in range(4):
                ps = wait_job(dve, f"hT{j}")
                if j >= 2:
                    settle()
                    dve.wait_ge(s["hT_high"], j - 1)
                w2 = cols[:, 2 * j:2 * j + 2].rearrange("p (k o) -> p k o", o=1).to_broadcast([P, 2, S])
                did(dve.tensor_tensor(tmp[:, j % 2].rearrange("p (k t) -> p k t", k=2), ps[:].rearrange("p (k t) -> p k t", k=2), w2, ALU.mult),
                    *job_read(f"hT{j}"))
                dve.wait_ge(s["hT_high"], j + 1)
                did(dve.tensor_tensor(flat(hTl, j), tmp[:, j % 2], flat(hTh, j).bitcast(F32), ALU.subtract), s["hT_ready"], j + 1)
                low_until(j)
            ps = wait_job(dve, "rel")
            did(dve.tensor_copy(rel8, ps[0:2 * H, 0:TW]), *job_read("rel"))
            dve.wait_ge(s["one_exp"], 1)
            did(dve.reciprocal(stat(OML, H), stat(ONE, H)))
            settle()
            did(dve.tensor_tensor(stat(OML, H), stat(OML, H), stat(ONE, H), ALU.mult))
            settle()
            did(dve.tensor_tensor(stat(LB, H), stat(OML, H), stat(OML, H), ALU.subtract))
            settle()
            did(dve.tensor_scalar(stat(OML, H), stat(LB, H), -1.0, 1.0, ALU.mult, ALU.add))
            dve.wait_ge(s["x_squares"], 4)
            parts = stat(OUT_P, 4).rearrange("p (t c) -> p t c", c=2)
            did(dve.tensor_tensor(stat(X_SS, 2), parts[:, :, 0], parts[:, :, 1], ALU.add), s["out_sums"], 1)
            low_until(9)

            dve.wait_ge(s["lat_rstd"], 1)
            for t in range(TT):
                did(dve.tensor_scalar(stage[:, 0, t, 0:RK], stage[:, 0, t, 0:RK], stat(LAT_RS + t), None, ALU.mult),
                    s["ckv_ready"], t + 1)
            low_until(11)
            dve.wait_ge(lvl_loaded, 16)
            did(dve.tensor_copy(lvl[:], prob[:, 0:len(LEVELS) * P]))
            after_block(dve, "idx")
            ik = stage[:, 1, :, 256:256 + DI]
            did(dve.tensor_reduce(stat(IK_MEAN, 2), ik, AX.X, ALU.add))
            settle()
            did(dve.tensor_scalar(stat(IK_MEAN, 2), stat(IK_MEAN, 2), -1.0 / DI, None, ALU.mult))
            settle()
            for t in range(TT):
                did(dve.tensor_scalar(ikc[:, t], stage[:, 1, t, 256:256 + DI], stat(IK_MEAN + t), None, ALU.add))
            did(dve.tensor_scalar(iws[:], stage[:, 1, :, 256 + DI:256 + DI + NI], NI ** -0.5, None, ALU.mult))
            settle()
            did(dve.tensor_tensor(ikn[:, :, 0:DI], ikc[:], ikc[:], ALU.mult))
            settle()
            did(dve.tensor_reduce(stat(IK_SS, 2), ikn[:, :, 0:DI], AX.X, ALU.add), s["ik_squares"], 1)
            low_until(12)
            dve.wait_ge(s["ik_rstd"], 1)
            settle()
            for t in range(TT):
                for c in range(2):
                    did(dve.tensor_scalar(ikn[:, t, c * DI:(c + 1) * DI], ikc[:, t], stat(IK_RS + t), None, ALU.mult),
                        s["ik_ready"], 2 * t + c + 1)
            ps = wait_job(dve, "ckvT")
            a = COLS["kv_norm"][0]
            did(dve.tensor_tensor(ckvT[:], heads(ps[:], RT), cols[:, a:a + RT].rearrange("p (k o) -> p k o", o=1).to_broadcast([P, RT, S]), ALU.mult),
                *job_read("ckvT"))
            low_until(14)
            ps = wait_job(dve, "ikT")
            did(dve.tensor_scalar(ikT[:], ps[:, 0:S], col("ik_w"), col("ik_b"), ALU.mult, ALU.add), *job_read("ikT"))
            low_until(17)

            def add_heads(i):
                after_job(dve, f"ix{i}")
                t, its_heads = INDEXER[i]
                w = 512 // len(its_heads)
                row = score[:, 0:P] if t == 0 else score[:, P:TW]
                for k, h in enumerate(its_heads):
                    part = relu[:, i % 2, k * w:(k + 1) * w]
                    settle()
                    if h == 0:
                        ins = dve.tensor_scalar(row, part, iws[:, t, h:h + 1], None, ALU.mult)
                    else:
                        ins = dve.scalar_tensor_tensor(out=row, in0=part, scalar=iws[:, t, h:h + 1], in1=row, op0=ALU.mult, op1=ALU.add)
                    if k == len(its_heads) - 1:
                        did(ins, s["relu_used"], i + 1)
                    else:
                        did(ins)

            for i in range(6):
                add_heads(i)
                if i % 2:
                    low_until(18 + i // 2)

            dve.wait_ge(s["score_ready"], 2)
            for r in range(NKEEP // 8):
                src = score if r == 0 else work
                for t, (a, z) in enumerate(((0, P), (P, TW))):
                    if r:
                        settle()
                    did(dve.max(top8[:, t], src[:, a:z]))
                    settle()
                    did(dve.match_replace(work[:, a:z], top8[:, t], src[:, a:z], TAKEN))
                if r in (1, 2, 4, 5):
                    low_until(20 + r)
                if r == 3:
                    after_job(dve, "hfT1")
                    for h in range(H):
                        did(dve.tensor_scalar(kT[:, h], kT[:, h], stat(OML + h), None, ALU.mult))
                        did(dve.tensor_scalar(pre[:, h], pre[:, h], stat(OML + h), stat(LB + h), ALU.mult, ALU.add))
                    settle()
                    did(dve.tensor_scalar(pre[:], pre[:], TINY, None, ALU.max), s["gates_ready"], 1)
            settle()
            did(dve.tensor_tensor(work[:], work[:], score[:], ALU.is_equal))

            def logits(pre_, k, head0):
                for i in range(3):
                    ps = wait_job(dve, f"{pre_}l{i}")
                    if i == 0:
                        bs = bias[:, head0:head0 + H, P:S]
                        dst = prob3[:, :, 0:P]
                        src = heads(ps[:])
                    else:
                        hh = 2 * (i - 1)
                        bs = bias[:, head0 + hh:head0 + hh + 2, :]
                        dst = prob3[:, hh:hh + 2, P:TW]
                        src = heads(ps[:], 2)
                    did(dve.scalar_tensor_tensor(out=dst, in0=src, scalar=SCALE, in1=bs, op0=ALU.mult, op1=ALU.add), *job_read(f"{pre_}l{i}"))

            def maxima(k):
                settle()
                did(dve.tensor_reduce(stat(NMAX + 8 * k, H), prob3[:, :, 0:P], AX.X, ALU.max, negate=True))
                did(dve.tensor_reduce(stat(NMAX + 8 * k + H, H), prob3[:, :, P:TW], AX.X, ALU.max, negate=True), s["logits_max"], k + 1)

            def normalise(k):
                dve.wait_ge(s["exp_done"], k + 1)
                did(dve.reciprocal(stat(RCP + 8 * k, 8), stat(SUM + 8 * k, 8)))
                settle()
                for t in range(TT):
                    for h in range(H):
                        row = prob3[:, h, 0:P] if t == 0 else prob3[:, h, P:TW]
                        ins = dve.tensor_scalar(row, row, stat(RCP + 8 * k + t * H + h), None, ALU.mult)
                        if t == TT - 1 and h == H - 1:
                            did(ins, s["prob_ready"], k + 1)
                        else:
                            did(ins)

            dve.wait_ge(bias_loaded, 16)
            logits("d", 0, H)
            low_until(24)
            settle()
            for t in range(TT):
                a, z = (0, P) if t == 0 else (P, TW)
                keep = work[:, a:z].rearrange("p (o k) -> p o k", o=1).to_broadcast([P, H, z - a])
                did(dve.scalar_tensor_tensor(out=prob3[:, :, a:z], in0=keep, scalar=NEG, in1=prob3[:, :, a:z], op0=ALU.mult, op1=ALU.add))
            maxima(0)
            low_until(26)

            eye_h = eye[:].rearrange("p (o k) -> p o k", o=1).to_broadcast([P, H, P])
            for t in range(TT):
                ps = wait_job(dve, f"diag{t}")
                did(dve.tensor_tensor(tri3[:, :, 2 * P * t:2 * P * t + P], heads(ps[:]), eye_h, ALU.mult), *job_read(f"diag{t}"))

            def level(i):
                settle()
                mask = lvl3[:, i:i + 1, :].to_broadcast([P, H, P])
                for t in range(TT):
                    name = f"L{LEVELS[i]}_{t}"
                    ps = wait_job(dve, name)
                    did(dve.copy_predicated(tri3[:, :, 2 * P * t:2 * P * t + P], mask, heads(ps[:])), *job_read(name))

            def y_low(jobs, b, k):
                for i, name in enumerate(jobs):
                    ps = wait_job(dve, name)
                    dve.wait_ge(s["y_high"], 2 * k + i + 1)
                    did(dve.tensor_tensor(flat(yl[b], i), ps[:, 0:512], flat(yh[b], i).bitcast(F32), ALU.subtract), *job_read(name))

            low_until(27)
            level(0)
            normalise(0)
            low_until(29)
            level(1)
            low_until(31)
            y_low(["dO0", "dO1"], 2, 0)
            low_until(32)
            level(2)
            low_until(34)
            level(3)
            low_until(36)
            level(4)
            low_until(38)
            level(5)
            logits("m", 1, 0)
            maxima(1)
            low_until(40)
            level(6)
            ps = wait_job(dve, "L128")
            did(dve.tensor_copy(tri3[:, :, P:2 * P], heads(ps[:])), *job_read("L128"))
            low_until(42)
            normalise(1)
            low_until(43)
            dve.wait_ge(hgn_loaded, 16)
            for t in range(TT):
                ps = wait_block(dve, "hg", t)
                dve.wait_ge(s["hg_sig"], t + 1)
                settle()
                did(dve.scalar_tensor_tensor(out=gw[:, t], in0=ps[:, 0:512], scalar=stat(X_RS + t), in1=gw[:, t], op0=ALU.mult, op1=ALU.mult),
                    *block_read("hg", t))
            for t in range(TT):
                settle()
                hgn_h = hgn[:].rearrange("p (o k) -> p o k", o=1).to_broadcast([P, H, P])
                did(dve.tensor_tensor(heads(gw[:, t]), heads(gw[:, t]), hgn_h, ALU.mult))
            low_until(45)
            for t in range(TT):
                dve.wait_ge(s["o_squares"], t + 1)
                did(dve.tensor_reduce(stat(O_SS + H * t, H), heads(relu[:, t]), AX.X, ALU.add), s["o_sums"], t + 1)
            low_until(46)
            dve.wait_ge(s["o_rstd"], 1)
            for t in range(TT):
                ps = wait_job(dve, f"ho{t}")
                for h in range(H):
                    settle()
                    ins = dve.scalar_tensor_tensor(out=stage[:, 1, t, h * P:(h + 1) * P], in0=ps[:, h * P:(h + 1) * P],
                                                   scalar=stat(O_RS + H * t + h), in1=gw[:, t, h * P:(h + 1) * P], op0=ALU.mult, op1=ALU.mult)
                    if h == H - 1:
                        did(ins, *job_read(f"ho{t}"))
                    else:
                        did(ins)
            low_until(47)
            y_low(["mO0", "mO1"], 1, 1)
            low_until(51)
            y_low(["yaT0", "yaT1"], 0, 2)

            n_merged = [0]

            def merge(c):
                for i, b in enumerate(BRANCHES):
                    low_until(LAST_UNIT[f"branch{b}{c}"] + 3)
                    after_block(dve, f"gate{b}{c}")
                    for t in range(TT):
                        ps = wait_block(dve, f"branch{b}{c}", t)
                        dst = merged[:, t, c * 512:(c + 1) * 512]
                        out_ = dst if i == 0 else tmp[:, t]
                        settle()
                        did(dve.tensor_tensor(out_, ps[:, 0:512], sig[:, b, t], ALU.mult), *block_read(f"branch{b}{c}", t))
                    settle()
                    if i:
                        for t in range(TT):
                            dst = merged[:, t, c * 512:(c + 1) * 512]
                            n_merged[0] += 1
                            did(dve.tensor_tensor(dst, dst, tmp[:, t], ALU.add), s["merged"], n_merged[0])

            def m_low(j):
                ps = wait_job(dve, f"mT{j}")
                dve.wait_ge(s["mT_high"], j + 1)
                did(dve.tensor_tensor(flat(mTl, j), ps[:, 0:512], flat(mTh, j).bitcast(F32), ALU.subtract), *job_read(f"mT{j}"))

            merge(0)
            low_until(FIRST_UNIT[f"gate{BRANCHES[0]}1"] + 4)
            m_low(0)
            m_low(1)
            merge(1)
            low_until(LAST_UNIT["branch01"] + 3)
            m_low(2)
            m_low(3)
            low_until(LAST_UNIT["out1"] + 5)

            dve.wait_ge(x1_loaded, 16)
            dve.wait_ge(post_loaded, 16)
            dve.wait_ge(s["out_squares"], 4)
            op = stat(OUT_P, 4).rearrange("p (t c) -> p t c", c=2)
            settle()
            did(dve.tensor_tensor(stat(OUT_SS, 2), op[:, :, 0], op[:, :, 1], ALU.add), s["out_sums"], 2)
            dve.wait_ge(s["out_rstd"], 1)
            for c in range(2):
                for t in range(TT):
                    ps = wait_block(dve, f"out{c}", t)
                    sl = slice(c * 512, (c + 1) * 512)
                    settle()
                    did(dve.scalar_tensor_tensor(out=mo[:, t, sl], in0=ps[:, 0:512], scalar=stat(OUT_RS + t), in1=post[:, sl],
                                                 op0=ALU.mult, op1=ALU.mult), *block_read(f"out{c}", t))
                    settle()
                    did(dve.tensor_tensor(x1[:, t, sl], x1[:, t, sl], mo[:, t, sl], ALU.add), s["x1_ready"], 2 * c + t + 1)
            for j in range(4):
                ps = wait_job(dve, f"h2T{j}")
                if j >= 2:
                    dve.wait_ge(s["h2_high"], j - 1)
                w2 = cols[:, 8 + 2 * j:10 + 2 * j].rearrange("p (k o) -> p k o", o=1).to_broadcast([P, 2, S])
                settle()
                did(dve.tensor_tensor(heads(fa[:, 0, j % 2], 2), heads(ps[:], 2), w2, ALU.mult), *job_read(f"h2T{j}"))
                dve.wait_ge(s["h2_high"], j + 1)
                did(dve.tensor_tensor(flat(hTl, j), fa[:, 0, j % 2], flat(hTh, j).bitcast(F32), ALU.subtract), s["h2_ready"], j + 1)

            def up(name, j, w, off):
                if j < 5:
                    after_block(dve, f"fg{j}")
                else:
                    dve.wait_ge(s["silu_last"], 2)
                if j >= 2:
                    wait_job(dve, f"fT{2 * (j - 2) + 1}")
                for t in range(TT):
                    ps = wait_block(dve, name, t)
                    settle()
                    did(dve.scalar_tensor_tensor(out=fa[:, j % 2, t, 0:w], in0=ps[:, off:off + w], scalar=stat(X1_RS + t),
                                                 in1=fg[:, j % 2, t, 0:w], op0=ALU.mult, op1=ALU.mult), *block_read(name, t))

            def f_low(j, n):
                for i in range(2 * j, 2 * j + n):
                    ps = wait_job(dve, f"fT{i}")
                    dve.wait_ge(s["fT_high"], i + 1)
                    did(dve.tensor_tensor(fT_l[:, 2 * i:2 * i + 2, :].rearrange("p k t -> p (k t)"), ps[:, 0:512],
                                          fT_h[:, 2 * i:2 * i + 2, :].rearrange("p k t -> p (k t)").bitcast(F32), ALU.subtract),
                        *job_read(f"fT{i}"))

            for j in range(5):
                if j:
                    low_until(LAST_UNIT[f"fu{j - 1}"] + 6)
                    f_low(j - 1, 2)
                low_until(LAST_UNIT[f"fu{j}"] + 4)
                up(f"fu{j}", j, 512, 0)
            low_until(LAST_UNIT["fu4"] + 6)
            f_low(4, 2)
            low_until(LAST_UNIT["fgu"] + 4)
            up("fgu", 5, 256, 256)
            low_until(LAST_UNIT["fgu"] + 7)
            f_low(5, 1)
            low_until(len(UNITS))
            dve.wait_ge(post_loaded, 32)
            for t in range(TT):
                dve.wait_ge(s["down_squares"], TT + t + 1)
                settle()
                did(dve.tensor_tensor(stat(DN_SS + t), stat(DN_P + 2 * t), stat(DN_P + 2 * t + 1), ALU.add), s["down_sums"], t + 1)
                dve.wait_ge(s["down_rstd"], t + 1)
                for c in range(2):
                    sl = slice(c * 512, (c + 1) * 512)
                    ps = wait_block(dve, f"down{c}", t)
                    settle()
                    did(dve.scalar_tensor_tensor(out=mo[:, t, sl], in0=ps[:, 0:512], scalar=stat(DN_RS + t), in1=post[:, sl],
                                                 op0=ALU.mult, op1=ALU.mult))
                settle()
                did(dve.tensor_tensor(mo[:, t], mo[:, t], x1[:, t], ALU.add), s["final_ready"], t + 1)

        @block.gpsimd
        def _(pool):
            last = [None]
            n_steps = [0]

            def did(ins, semaphore=None, value=None):
                if semaphore is None:
                    n_steps[0] += 1
                    semaphore, value = pool_step, n_steps[0]
                ins.then_inc(semaphore, 1)
                last[0] = (semaphore, value)

            def settle():
                pool.wait_ge(*last[0])

            did(pool.memset(rel[BUCKETS:BUCKETS + 1, :], NEG), rel_row, 1)
            settle()
            did(pool.memset(suf[:], 1.0))
            settle()
            did(pool.memset(stat(HALF, 8), -0.5))
            settle()

            def rstd(dst, src, n, count, done, value=1):
                settle()
                did(pool.tensor_scalar(stat(RMS_TMP, n), stat(src, n), 1.0 / count, EPS, ALU.mult, ALU.add))
                settle()
                did(pool.tensor_tensor(stat(dst, n), stat(RMS_TMP, n), stat(HALF, n), ALU.pow), done, value)

            pool.wait_ge(s["out_sums"], 1)
            rstd(X_RS, X_SS, 2, D, s["x_rstd"])
            pool.wait_ge(s["lat_squares"], 2)
            rstd(LAT_RS, LAT_SS, 2, RK, s["lat_rstd"])
            pool.wait_ge(s["ik_squares"], 1)
            rstd(IK_RS, IK_SS, 2, DI, s["ik_rstd"])
            for t in range(TT):
                pool.wait_ge(s["relu_used"], 2 if t == 0 else 6)
                diag = score[:, 0:P] if t == 0 else score[:, 2 * P:TW]
                did(pool.affine_select(out=diag, in_=diag, compare_op=ALU.is_ge, fill=NEG, base=0,
                                       pattern=[[-1, P]], channel_multiplier=1), s["score_ready"], t + 1)

            pool.wait_ge(s["gates_ready"], 1)
            after_job(pool, "hqT1")

            def halves(ap, w):
                v = ap.rearrange("p h t -> p (h t)").rearrange("p (g two s) -> p g two s", two=2, s=w)
                return v[:, :, 0, :], v[:, :, 1, :]

            for i, w in enumerate(LEVELS + [P]):
                g = H * S // (2 * w)
                a_lo, a_up = halves(att[i % 2], w)
                k_lo, _ = halves(kT[:], w)
                _, q_up = halves(hqT[:], w)
                p_lo, p_up = halves(pre[:], w)
                s_lo, s_up = halves(suf[:], w)
                if i >= 2:
                    wait_job(pool, f"L{LEVELS[i - 2]}_1")
                did(pool.tensor_tensor(a_lo, k_lo, s_lo, ALU.mult))
                did(pool.tensor_tensor(a_up, q_up, p_up, ALU.mult), s["level_built"], i + 1)
                settle()
                if w < P:
                    did(pool.tensor_tensor(s_lo, s_lo, p_up[:, :, w - 1:w].to_broadcast([P, g, w]), ALU.mult))
                    settle()
                    did(pool.tensor_tensor(p_up, p_up, p_lo[:, :, w - 1:w].to_broadcast([P, g, w]), ALU.mult))
                    settle()
            pool.wait_ge(s["o_sums"], 2)
            rstd(O_RS, O_SS, 8, P, s["o_rstd"])
            pool.wait_ge(s["out_sums"], 2)
            rstd(OUT_RS, OUT_SS, 2, D, s["out_rstd"])
            pool.wait_ge(s["x1_squares"], 2)
            rstd(X1_RS, X1_SS, 2, D, s["h2_rstd"])
            for t in range(TT):
                pool.wait_ge(s["down_sums"], t + 1)
                rstd(DN_RS + t, DN_SS + t, 1, D, s["down_rstd"], t + 1)

        @block.tensor
        def _(pe):
            next_unit = [0]
            next_job = [0]

            def begin(name):
                assert JOBS[next_job[0]] == name, (JOBS[next_job[0]], name)
                next_job[0] += 1
                b, n = job_bank(name)
                if n:
                    pe.wait_ge(bank_read[b], n)
                return bank[b]

            def end(name, ins):
                ins.then_inc(bank_full[job_bank(name)[0]], 1)

            def lhs_of(name):
                if name.startswith("branch"):
                    b = int(name[6])
                    return yh[b], yl[b]
                if name.startswith("out"):
                    return mTh, mTl
                if name.startswith("down"):
                    return fT_h, fT_l
                return hTh, hTl

            def units(u_end):
                while next_unit[0] <= u_end:
                    u = next_unit[0]
                    b, kt0, w = UNITS[u]
                    name, n_kt, _ = BLOCKS[b]
                    high, low = lhs_of(name)
                    pe.wait_ge(low_done, u + 1)
                    slot = u % SPLIT
                    rh = wh[:, slot, 0:2 * w].rearrange("p (k n) -> p k n", k=2)
                    rl = wl[:, slot, 0:2 * w].rearrange("p (k n) -> p k n", k=2)
                    for t in range(TT):
                        bk, n = block_bank(name, t)
                        if kt0 == 0 and n:
                            pe.wait_ge(bank_read[bk], n)
                        for k in range(2):
                            kt = kt0 + k
                            for lhs, rhs in ((high, rh), (high, rl), (low, rh)):
                                first = kt == 0 and lhs is high and rhs is rh
                                final = kt == n_kt - 1 and lhs is low
                                ins = pe.matmul(bank[bk][:, 0:w], lhs[:, kt, t * P:(t + 1) * P], rhs[:, k], start=first, stop=final)
                                if final:
                                    ins.then_inc(bank_full[bk], 1)
                    if kt0 + 2 < n_kt:
                        ins.then_inc(unit_used, 1)
                    next_unit[0] += 1

            def transposes(name, sources):
                ps = begin(name)
                for i, src in enumerate(sources):
                    ins = pe.transpose(ps[:, i * P:(i + 1) * P], src, eye[:])
                end(name, ins)

            def tiles(src, h0=None):
                return [src[:, t, (h0 + k) * P:(h0 + k + 1) * P] for k in range(2) for t in range(TT)]

            pe.wait_ge(eye_loaded, 16)
            pe.wait_ge(x_loaded, 32)
            for j in range(4):
                transposes(f"hT{j}", tiles(x0, 2 * j))
            pe.wait_ge(rel_loaded, 32)
            pe.wait_ge(rel_row, 1)
            ps = begin("rel")
            end("rel", pe.matmul(ps[0:2 * H, 0:TW], rel[:], hot, start=True, stop=True))
            for j in range(4):
                pe.wait_ge(s["hT_ready"], j + 1)
                units(j)
            units(8)
            pe.wait_ge(s["ckv_ready"], 2)
            transposes("ckvT", [stage[:, 0, t, k * P:(k + 1) * P] for k in range(RT) for t in range(TT)])
            transposes("iqT0", tiles(stage[:, 0], 2))
            units(10)
            after_block(pe, "idx")
            transposes("iqT1", tiles(stage[:, 1], 0))
            pe.wait_ge(s["ik_ready"], 4)
            transposes("ikT", [ikn[:, t] for t in range(TT)])
            units(11)
            after_job(pe, "ckvT")
            pe.wait_ge(lat_loaded, 32)
            for i in range(2):
                ps = begin(f"kc{i}")
                for k in range(2):
                    h = 2 * i + k
                    for r in range(RT):
                        ins = pe.matmul(ps[:, k * S:(k + 1) * S], wuk[:, r, h * P:(h + 1) * P], ckvT[:, r, :], start=r == 0, stop=r == RT - 1)
                end(f"kc{i}", ins)
            units(12)
            for t in range(TT):
                ps = begin(f"vc{t}")
                for r in range(RT):
                    ins = pe.matmul(ps[:], ckvT[:, r, t * P:(t + 1) * P], wuv[:, r, :], start=r == 0, stop=r == RT - 1)
                end(f"vc{t}", ins)
            after_job(pe, "iqT1")
            after_job(pe, "ikT")
            for i in range(6):
                if i % 2 == 0:
                    units(13 + i // 2)
                ps = begin(f"ix{i}")
                t, its_heads = INDEXER[i]
                w = 512 // len(its_heads)
                for k, h in enumerate(its_heads):
                    b = DI * (h % 2)
                    ins = pe.matmul(ps[:, k * w:(k + 1) * w], iqT[b:b + DI, h // 2, t * P:(t + 1) * P], ikT[b:b + DI, 0:w], start=True, stop=True)
                end(f"ix{i}", ins)
            units(16)
            after_block(pe, "dq")
            for i in range(2):
                transposes(f"dqT{i}", tiles(stage[:, 2], 2 * i))
            units(18)
            after_block(pe, "hf")
            for i in range(2):
                transposes(f"hfT{i}", tiles(stage[:, 0], 2 * i))

            def logits(kind):
                for i in range(3):
                    ps = begin(f"{kind}l{i}")
                    for k in range(H if i == 0 else 2):
                        h = k if i == 0 else 2 * (i - 1) + k
                        t, w = (0, P) if i == 0 else (1, S)
                        ins = pe.matmul(ps[:, k * w:(k + 1) * w], qT[:, h, t * P:(t + 1) * P], kcT[:, h, 0:w], start=True, stop=True)
                    end(f"{kind}l{i}", ins)

            def prob_transposes(kind):
                for i in range(3):
                    transposes(f"{kind}P{i}", [prob[:, (4 * i + k) * P:(4 * i + k + 1) * P] for k in range(4)])

            def values(kind, v):
                for i in range(2):
                    ps = begin(f"{kind}O{i}")
                    for k in range(2):
                        h = 2 * i + k
                        pe.matmul(ps[:, k * S:(k + 1) * S], v[:, 0, h * P:(h + 1) * P], probT3[:, h, 0:S], start=True, stop=False)
                        ins = pe.matmul(ps[:, k * S + P:(k + 1) * S], v[:, 1, h * P:(h + 1) * P], probT3[:, h, S:TW], start=False, stop=True)
                    end(f"{kind}O{i}", ins)

            after_job(pe, "dqT1")
            after_job(pe, "kc1")
            logits("d")
            units(22)
            after_block(pe, "hq")
            for i in range(2):
                transposes(f"hqT{i}", tiles(stage[:, 1], 2 * i))
            units(23)
            after_job(pe, "hqT1")
            pe.wait_ge(s["gates_ready"], 1)
            for t in range(TT):
                ps = begin(f"diag{t}")
                for h in range(H):
                    ins = pe.matmul(ps[:, h * P:(h + 1) * P], kT[:, h, t * P:(t + 1) * P], hqT[:, h, t * P:(t + 1) * P], start=True, stop=True)
                end(f"diag{t}", ins)

            def level(i):
                pe.wait_ge(s["level_built"], i + 1)
                for t in range(TT):
                    name = f"L{LEVELS[i]}_{t}"
                    ps = begin(name)
                    for h in range(H):
                        a_h = att[i % 2][:, h, t * P:(t + 1) * P]
                        ins = pe.matmul(ps[:, h * P:(h + 1) * P], a_h, a_h, start=True, stop=True)
                    end(name, ins)

            units(24)
            level(0)
            units(25)
            pe.wait_ge(s["prob_ready"], 1)
            prob_transposes("d")
            units(26)
            level(1)
            units(27)
            after_job(pe, "dP2")
            after_job(pe, "vc1")
            values("d", vc)
            units(28)
            level(2)
            units(29)
            after_block(pe, "mq")
            for i in range(2):
                transposes(f"mqT{i}", tiles(stage[:, 2], 2 * i))
            units(30)
            level(3)
            units(32)
            level(4)
            units(33)
            after_block(pe, "mk")
            for i in range(2):
                transposes(f"mkT{i}", tiles(stage[:, 0], 2 * i))
            units(34)
            level(5)
            after_job(pe, "mqT1")
            after_job(pe, "mkT1")
            logits("m")
            units(36)
            level(6)
            units(38)
            pe.wait_ge(s["level_built"], len(LEVELS) + 1)
            ps = begin("L128")
            for h in range(H):
                a_h = att[len(LEVELS) % 2][:, h, :]
                ins = pe.matmul(ps[:, h * P:(h + 1) * P], a_h[:, 0:P], a_h[:, P:S], start=True, stop=True)
            end("L128", ins)
            units(40)
            pe.wait_ge(s["prob_ready"], 2)
            prob_transposes("m")
            units(41)
            after_job(pe, "L128")
            after_block(pe, "hi")
            for t in range(TT):
                ps = begin(f"ho{t}")
                for h in range(H):
                    hs = slice(h * P, (h + 1) * P)
                    if t == 0:
                        ins = pe.matmul(ps[:, hs], tri3[:, h, 0:P], hv[:, 0, hs], start=True, stop=True)
                    else:
                        pe.matmul(ps[:, hs], tri3[:, h, P:2 * P], hv[:, 0, hs], start=True, stop=False)
                        ins = pe.matmul(ps[:, hs], tri3[:, h, 2 * P:TW], hv[:, 1, hs], start=False, stop=True)
                end(f"ho{t}", ins)
            units(42)
            after_job(pe, "mP2")
            after_block(pe, "mv")
            values("m", mv)
            units(47)
            after_job(pe, "ho1")
            for i in range(2):
                transposes(f"yaT{i}", tiles(stage[:, 1], 2 * i))
            for c in range(2):
                if c == 1:
                    units(FIRST_UNIT[f"gate{BRANCHES[0]}1"] + 2)
                    pe.wait_ge(s["merged"], 4)
                    for j in range(2):
                        transposes(f"mT{j}", tiles(merged, 2 * j))
                units(LAST_UNIT[f"gate{BRANCHES[2]}{c}"])
                if c == 0:
                    after_job(pe, "mO1")
                    after_job(pe, "dO1")
                    after_job(pe, "yaT1")
                units(LAST_UNIT[f"branch{BRANCHES[2]}{c}"])
            after_job(pe, "mT1")
            units(FIRST_UNIT["out0"] + 1)
            pe.wait_ge(s["merged"], 8)
            for j in range(2, 4):
                transposes(f"mT{j}", tiles(merged, 2 * j))
            after_job(pe, "mT3")
            units(LAST_UNIT["out1"])
            for j in range(4):
                pe.wait_ge(s["x1_ready"], 2 if j < 2 else 4)
                transposes(f"h2T{j}", tiles(x1, 2 * j))
            for j in range(4):
                pe.wait_ge(s["h2_ready"], j + 1)
                units(FIRST_UNIT["fg0"] + j)
            for j in range(5):
                if j:
                    units(LAST_UNIT[f"fu{j - 1}"] + 2)
                    after_block(pe, f"fu{j - 1}")
                    for i in range(2):
                        transposes(f"fT{2 * (j - 1) + i}", tiles(fa[:, (j - 1) % 2], 2 * i))
                units(LAST_UNIT[f"fu{j}"])
            units(LAST_UNIT["fu4"] + 2)
            after_block(pe, "fu4")
            for i in range(2):
                transposes(f"fT{8 + i}", tiles(fa[:, 0], 2 * i))
            units(LAST_UNIT["fgu"])
            after_job(pe, "fT9")
            units(LAST_UNIT["fgu"] + 3)
            after_block(pe, "fgu")
            transposes("fT10", tiles(fa[:, 1], 0))
            units(LAST_UNIT["down0"] - 1)
            after_job(pe, "fT10")
            units(LAST_UNIT["down1"])


def weight_stream(w_in, w_branch, w_out, w_ffn_in, w_ffn_out):
    start = {n: c for n, c, _ in IN_BLOCKS}
    parts = []
    for b, kt, w in UNITS:
        name = BLOCKS[b][0]
        if name in start:
            pieces = [(w_in, start[name], w)]
        elif name.startswith("gate"):
            pieces = [(w_in, C_G + int(name[4]) * D + int(name[5]) * 512, 512)]
        elif name.startswith("branch"):
            pieces = [(w_branch[int(name[6])], int(name[7]) * 512, 512)]
        elif name.startswith("out"):
            pieces = [(w_out, int(name[3]) * 512, 512)]
        elif name == "fgu":
            pieces = [(w_ffn_in, 5 * 512, 256), (w_ffn_in, DFF + 5 * 512, 256)]
        elif name.startswith("fg"):
            pieces = [(w_ffn_in, int(name[2]) * 512, 512)]
        elif name.startswith("fu"):
            pieces = [(w_ffn_in, DFF + int(name[2]) * 512, 512)]
        else:
            pieces = [(w_ffn_out, int(name[4]) * 512, 512)]
        rows = slice(kt * P, (kt + 2) * P)
        unit = np.concatenate([m[rows, c:c + n] for m, c, n in pieces], axis=1)
        parts.append(unit.reshape(2, P, w).transpose(1, 0, 2).reshape(-1))
    return np.concatenate(parts)


def kernel(x, w_in, pre_mix_norm, post_mix_norm, pre_ffn_norm, post_ffn_norm, hg_lb_logits, hg_norm_w, dsa_kv_norm,
           dsa_w_uk, dsa_w_uv, idx_k_norm_w, idx_k_norm_b, rel_bias, w_branch_a, w_branch_b, w_branch_c, w_out,
           w_ffn_in, w_ffn_out):
    import concourse.bacc as bacc
    from concourse.bass_utils import run_bass_kernel_spmd

    w_in, w_out, w_ffn_in, w_ffn_out = (np.asarray(a)[0] for a in (w_in, w_out, w_ffn_in, w_ffn_out))
    w_branch = [np.asarray(a)[0] for a in (w_branch_a, w_branch_b, w_branch_c)]

    def by_partition(a):
        return np.asarray(a).reshape(-1, P).T

    def twice(a):
        return np.concatenate([np.asarray(a).reshape(DI, 1)] * 2)

    eye, levels, hot = constants()
    arrays = {
        "w_stream": weight_stream(w_in, w_branch, w_out, w_ffn_in, w_ffn_out),
        "x_in": np.ascontiguousarray(x),
        "cols_in": np.ascontiguousarray(np.concatenate(
            [by_partition(pre_mix_norm), by_partition(pre_ffn_norm), by_partition(hg_lb_logits), by_partition(dsa_kv_norm),
             twice(idx_k_norm_w), twice(idx_k_norm_b)], axis=1)),
        "eye_in": eye, "levels_in": levels, "hot_in": hot,
        "rel_in": np.ascontiguousarray(np.concatenate([np.asarray(rel_bias)], axis=1)),
        "w_uk": np.ascontiguousarray(dsa_w_uk).reshape(RK, HW),
        "w_uv": np.ascontiguousarray(dsa_w_uv).reshape(RK, HW),
        "hg_norm": np.ascontiguousarray(hg_norm_w),
        "post_mix": np.ascontiguousarray(post_mix_norm),
        "post_ffn": np.ascontiguousarray(post_ffn_norm),
    }
    nc = bacc.Bacc("TRN2", target_bir_lowering=False, num_devices=1, dynamic_dma_scratch_size=1024)
    args = {n: nc.dram_tensor(n, a.shape, mybir.dt.from_np(a.dtype), kind="ExternalInput").ap() for n, a in arrays.items()}
    out = nc.dram_tensor("out", (1, S, D), F32, kind="ExternalOutput").ap()
    build_block(nc, **args, out=out)
    r = run_bass_kernel_spmd(nc, [arrays], core_ids=[0])
    return r.results[0]["out"]
```

```python
from contextlib import ExitStack

import concourse.bass as bass
import numpy as np
from concourse import mybir

F32 = mybir.dt.float32
F32R = mybir.dt.float32r
U8 = mybir.dt.uint8
ALU = mybir.AluOpType
ACT = mybir.ActivationFunctionType
AX = mybir.AxisListType

P = 128
D = 1024
S = 256
TT = S // P
KT = D // P
H = 4
HW = H * P
NI, DI = 8, 64
RK = 256
RT = RK // P
DFF = 2816
FT = DFF // P
NKEEP = 64
EPS, NEG, TINY = 1e-6, -1e30, 1e-20
TAKEN = -3e38
SCALE = float(P) ** -0.5
ROOT = float(D) ** -0.5
BUCKETS, TW, SKEW = 32, 384, 16

C_HQ, C_HF, C_HI, C_HG, C_MQ, C_MK, C_MV, C_DQ, C_CKV, C_IW_END, C_G = (
    0, 512, 1024, 1536, 2048, 2560, 3072, 3584, 4096, 4936, 4936)

IN_BLOCKS = [("lat", C_CKV, 512), ("idx", C_CKV + 512, C_IW_END - C_CKV - 512), ("dq", C_DQ, 512),
             ("hf", C_HF, 512), ("hq", C_HQ, 512), ("hi", C_HI, 512), ("mq", C_MQ, 512), ("mk", C_MK, 512),
             ("mv", C_MV, 512), ("hg", C_HG, 512)]
BRANCHES = (1, 2, 0)


def plan_blocks():
    blocks = [(n, KT, w) for n, _, w in IN_BLOCKS]
    for c in range(2):
        blocks += [(f"gate{b}{c}", KT, 512) for b in BRANCHES]
        blocks += [(f"branch{b}{c}", H, 512) for b in BRANCHES]
    blocks += [(f"out{c}", KT, 512) for c in range(2)]
    for j in range(DFF // 512):
        blocks += [(f"fg{j}", KT, 512), (f"fu{j}", KT, 512)]
    blocks += [("fgu", KT, 512)]
    blocks += [(f"down{c}", FT, 512) for c in range(2)]
    blocks += [("uk", RT, HW), ("uv", RT, HW)]
    return blocks


BLOCKS = plan_blocks()
BLOCK = {n: b for b, (n, _, _) in enumerate(BLOCKS)}


def plan_units():
    units = []
    for b, (name, n, w) in enumerate(BLOCKS):
        if name == "out0":
            units += [(b + c, kt + k, w) for kt in (0, n // 2) for c in range(2) for k in range(0, n // 2, 2)]
        elif name != "out1":
            units += [(b, kt, w) for kt in range(0, n, 2)]
        if name == "dq":
            units += [(BLOCK["uk"], 0, HW), (BLOCK["uv"], 0, HW)]
    return units[:-2]


UNITS = plan_units()
OFFSETS = [int(v) for v in np.cumsum([0] + [P * 2 * w for _, _, w in UNITS])]
LAST_UNIT = {BLOCKS[b][0]: u for u, (b, _, _) in enumerate(UNITS)}
FIRST_UNIT = {BLOCKS[b][0]: u for u, (b, _, _) in reversed(list(enumerate(UNITS)))}

NOT_LAST = list(int(v) for v in np.cumsum([kt + 2 != BLOCKS[b][1] for b, kt, _ in UNITS]))

RAW, SPLIT = 4, 6

LEVELS = [1, 2, 4, 8, 16, 32, 64]
JOBS = (["hT00", "hT01", "hT10", "hT11", "rel", "ckvT", "iqT0", "iqT1", "kc0", "kc1", "vc0", "vc1", "ikT"]
        + [f"ix{i}" for i in range(6)] + ["dqT0", "dqT1", "hfT0", "hfT1", "hqT0", "hqT1",
                                          "diag0", "diag1", "dl0", "dl1", "dl2", "L1", "L2", "L4", "dP0", "dP1", "dP2", "L8",
                                          "dO0", "dO1", "mqT0", "mqT1", "L16", "L32",
                                          "mkT0", "mkT1", "ml0", "ml1", "ml2", "L64", "L128",
                                          "mP0", "mP1", "mP2", "ho0", "ho1", "mO0", "mO1", "yaT0", "yaT1",
                                          "mT0", "mT1", "mT2", "mT3", "h2T00", "h2T01", "h2T10", "h2T11"]
        + [f"fT{i}" for i in range(FT // 2)])
JOB = {n: m for m, n in enumerate(JOBS)}
INDEXER = [(0, (0, 2, 4, 6)), (0, (1, 3, 5, 7)), (1, (0, 2)), (1, (4, 6)), (1, (1, 3)), (1, (5, 7))]


def bias_runs():
    n = np.arange(S)
    half = BUCKETS // 2
    nf = np.maximum(n, half).astype(np.float32)
    large = half + (np.log(nf / half) / np.log(2048 / half) * (BUCKETS - half)).astype(np.int32)
    return np.where(n < half, n, np.minimum(large, BUCKETS - 1))


def constants():
    eye = np.eye(P, dtype=np.float32)
    i, j = np.arange(P)[None, :], np.arange(P)[:, None]
    levels = np.stack([((i // (2 * s)) == (j // (2 * s)))[:, np.arange(P) // s % 2 == 1] & ((j // s) % 2 == 0)
                       for s in LEVELS], 1).astype(np.float32)
    hot = np.zeros((BUCKETS + 1, TW), np.float32)
    bucket = bias_runs()
    for m in range(TW):
        dist = S - 1 - m
        hot[bucket[dist] if dist >= 0 else BUCKETS, m] = 1.0
    return eye, np.ascontiguousarray(levels.reshape(P, -1)), hot


COLS = {"pre_mix": (0, 8), "lb": (8, 12), "kv_norm": (12, 14), "ik_w": (14, 15), "ik_b": (15, 16)}
NCOLS = 16


def build_block(nc, w_stream, x_in, cols_in, eye_in, levels_in, hot_in, rel_in,
                hg_norm, post_mix, pre_ffn, post_ffn, out):
    ctx = ExitStack()
    with ctx:
        def sb(name, shape, dt=F32, stack=ctx):
            return stack.enter_context(nc.sbuf_tensor(name, shape, dt))

        def sem(name):
            return ctx.enter_context(nc.semaphore(name))

        raw = sb("raw", [P, RAW, 1024])
        wh = sb("wh", [P, SPLIT, 1024], F32R)
        wl = sb("wl", [P, SPLIT, 1024], F32R)
        hTh = sb("hTh", [P, KT, S], F32R)
        hTl = sb("hTl", [P, KT, S], F32R)
        eye = sb("eye", [P, P])
        cols = sb("cols", [P, NCOLS])
        st = sb("st", [P, 160])
        post = sb("post", [P, D])
        tmp = sb("tmp", [P, 2, 512])
        sig = sb("sig", [P, 3, TT, 512])
        yh = [sb(f"yh{b}", [P, H, S], F32R) for b in range(3)]
        yl = [sb(f"yl{b}", [P, H, S], F32R) for b in range(3)]

        early = ExitStack()
        x0 = sb("x0", [P, TT, D], stack=early)
        stage = sb("stage", [P, 3, TT, 512], stack=early)
        ikn = sb("ikn", [P, TT, P], stack=early)
        ikc = sb("ikc", [P, TT, DI], stack=early)
        iws = sb("iws", [P, TT, NI], stack=early)
        ckvT = sb("ckvT", [P, RT, S], stack=early)
        ikT = sb("ikT", [P, S], stack=early)
        ckvh, ckvl = yh[0][:, 0:RT], yl[0][:, 0:RT]
        hqT = sb("hqT", [P, H, S], stack=early)
        iqT = hqT
        kT = sb("kT", [P, H, S], stack=early)
        pre = sb("pre", [P, H, S], stack=early)
        suf = sb("suf", [P, H, S], stack=early)
        att = [sb(f"att{i}", [P, H, S], stack=early) for i in range(2)]
        tri = sb("tri", [P, H, TW], stack=early)
        qT = sb("qT", [P, H, S], stack=early)
        kcT = sb("kcT", [P, H, S], stack=early)
        vc = sb("vc", [P, TT, HW], stack=early)
        mv = sb("mv", [P, TT, HW], stack=early)
        hv = x0[:, 0].rearrange("p (t n) -> p t n", t=TT)
        gw = x0[:, 1].rearrange("p (t n) -> p t n", t=TT)
        bias = sb("bias", [P, 2 * H, S], stack=early)
        prob = sb("prob", [P, H * TW], stack=early)
        probT = sb("probT", [P, H * TW], stack=early)
        rel = sb("rel", [BUCKETS + 1, 2 * H], stack=early)
        relu = tmp
        score = sb("score", [P, TW], stack=early)
        work = sb("work", [P, TW], stack=early)
        rel8 = score[0:2 * H]
        hot = work[0:BUCKETS + 1]
        top8 = sb("top8", [P, 2, 8], stack=early)
        lvl = sb("lvl", [P, len(LEVELS) * P // 2], U8, stack=early)
        hgn = sb("hgn", [P, P], stack=early)
        early.close()
        late = ExitStack()
        x1 = sb("x1", [P, TT, D], stack=late)
        mo = sb("mo", [P, TT, D], stack=late)
        fg = sb("fg", [P, 2, TT, 512], stack=late)
        fa = sb("fa", [P, 2, TT, 512], stack=late)
        wf, pw = (fg[:, k].rearrange("p t n -> p (t n)") for k in range(2))
        merging = ExitStack()
        mTh = sb("mTh", [P, KT, S], F32R, stack=merging)
        mTl = sb("mTl", [P, KT, S], F32R, stack=merging)
        merged = sb("merged", [P, TT, D], stack=merging)
        h2 = sb("h2", [P, TT, D], stack=merging)
        mow = sb("mow", [P, TT, D], stack=merging)
        merging.close()
        fT_h = sb("fTh", [P, FT, S], F32R, stack=late)
        fT_l = sb("fTl", [P, FT, S], F32R, stack=late)
        late.close()

        bank = [ctx.enter_context(nc.psum_tensor(f"bank{b}", [P, 512], F32)) for b in range(8)]
        scratch = nc.dram_tensor("bias_scratch", [2 * H * SKEW * TW], F32, kind="Internal").ap()

        raw_loaded = [sem(f"raw_loaded{i}") for i in range(RAW)]
        high_done, low_done, unit_used = sem("high_done"), sem("low_done"), sem("unit_used")
        hT1_ready, half_set = sem("hT1_ready"), sem("half_set")
        bank_full = [sem(f"bank_full{b}") for b in range(8)]
        bank_read = [sem(f"bank_read{b}") for b in range(8)]
        x_loaded = [sem("x_loaded0"), sem("x_loaded1")]
        eye_loaded, cols_loaded = sem("eye_loaded"), sem("cols_loaded")
        rel_loaded, post_loaded, hgn_loaded = sem("rel_loaded"), sem("post_loaded"), sem("hgn_loaded")
        x1_loaded, lvl_loaded = sem("x1_loaded"), sem("lvl_loaded")
        rel_row, rel_stored, bias_loaded = sem("rel_row"), sem("rel_stored"), sem("bias_loaded")
        act_step, dve_step, pool_step = sem("act_step"), sem("dve_step"), sem("pool_step")
        names = """
            ckv_high ckv_low ckv_ready down_mean down_rstd down_squares exp_done fT_high final_ready
            gates_ready h2_high h2_input h2_rstd hT_high hT_ready hg_sig ik_ready ik_rstd ik_squares
            lat_rstd lat_squares lb_delta level_built logits_max mT_high merged o_rstd o_squares
            o_sums one_exp out_mean out_rstd out_squares out_sums prob_ready relu_used score_ready
            silu_last stored x1_ready x1_squares x_rstd x_squares y_high
        """.split()
        s = {n: sem(n) for n in names}

        def block_bank(name, t):
            n = BLOCK[name]
            return 2 * (n % 2) + t, n // 2

        def job_bank(name):
            m = JOB[name]
            return 4 + m % 4, m // 4

        def wait_block(eng, name, t):
            b, n = block_bank(name, t)
            eng.wait_ge(bank_full[b], n + 1)
            return bank[b]

        def wait_job(eng, name):
            b, n = job_bank(name)
            eng.wait_ge(bank_full[b], n + 1)
            return bank[b]

        def block_read(name, t):
            b, n = block_bank(name, t)
            return bank_read[b], n + 1

        def job_read(name):
            b, n = job_bank(name)
            return bank_read[b], n + 1

        def after_job(eng, name):
            eng.wait_ge(*job_read(name))

        def after_block(eng, name):
            eng.wait_ge(*block_read(name, TT - 1))

        def wait_unit_used(eng, u):
            b, kt, _ = UNITS[u]
            name, n_kt, _ = BLOCKS[b]
            if kt + 2 == n_kt:
                if name in ("uk", "uv"):
                    wait_job(eng, "kc1" if name == "uk" else "vc1")
                else:
                    wait_block(eng, name, TT - 1)
            else:
                eng.wait_ge(unit_used, NOT_LAST[u])

        X_SS, X_RS, LAT_SS, LAT_RS, IK_MEAN, IK_SS, IK_RS = 0, 2, 4, 6, 8, 10, 12
        LB, OML, ONE = 16, 20, 24
        NMAX, SUM, RCP = 28, 44, 60
        O_SS, O_RS = 76, 84
        OUT_P, OUT_SS, OUT_RS, X1_SS, X1_RS = 92, 96, 98, 100, 102
        DN_P, DN_SS, DN_RS = 104, 108, 110
        HALF, RMS_TMP, ZERO = 112, 120, 130

        def col(name, i=0):
            a = COLS[name][0] + i
            return cols[:, a:a + 1]

        def stat(i, n=1):
            return st[:, i:i + n]

        tri3 = tri[:]
        prob3 = prob[:].rearrange("p (h k) -> p h k", h=H)
        probT3 = probT[:].rearrange("p (h k) -> p h k", h=H)
        lvl3 = lvl[:].rearrange("p (l k) -> p l k", l=len(LEVELS))

        def half_kt(ap, t, j):
            return ap[:, 4 * j:4 * j + 4, t * P:(t + 1) * P]

        def heads(ap, n=H):
            return ap.rearrange("p (h k) -> p h k", h=n)

        block = ctx.enter_context(nc.Block())

        @block.sync
        def _(sp):
            x_rows = x_in.rearrange("o (t p) d -> p (o t) d", p=P)
            sp.dma_start(x0[:, 0], x_rows[:, 0]).then_inc(x_loaded[0], 16)
            sp.dma_start(cols[:], cols_in).then_inc(cols_loaded, 16)
            sp.dma_start(x0[:, 1], x_rows[:, 1]).then_inc(x_loaded[1], 16)
            for u, (b, kt, w) in enumerate(UNITS):
                if u >= RAW:
                    sp.wait_ge(low_done, u - RAW + 1)
                src = w_stream[OFFSETS[u]:OFFSETS[u + 1]].rearrange("(p n) -> p n", p=P)
                sp.dma_start(raw[:, u % RAW, 0:2 * w], src).then_inc(raw_loaded[u % RAW], 16)
                if u == 8:
                    after_job(sp, "rel")
                    rows = rel8.rearrange("h (o m) -> h o m", o=1).to_broadcast([2 * H, SKEW, TW])
                    sp.dma_start(scratch.rearrange("(h p m) -> h p m", h=2 * H, p=SKEW), rows).then_inc(rel_stored, 16)
                if u == 14:
                    sp.wait_ge(rel_stored, 16)
                    for q in range(0, P, SKEW):
                        skewed = bass.AP(scratch.tensor, P - 1 - q, [[TW - 1, SKEW], [SKEW * TW, 2 * H], [1, S]])
                        sp.dma_start(bias[q:q + SKEW], skewed).then_inc(bias_loaded, 16)
                if u == FIRST_UNIT["branch11"] - 1:
                    sp.wait_ge(s["merged"], 4)
                    sp.dma_start(x1[:], x_rows).then_inc(x1_loaded, 16)
                    sp.dma_start(wf, pre_ffn.to_broadcast([P, D])).then_inc(x1_loaded, 16)
                if u == LAST_UNIT["down0"]:
                    sp.wait_ge(s["x1_ready"], TT)
                    sp.dma_start(post[:], post_ffn.to_broadcast([P, D])).then_inc(post_loaded, 16)
            y_rows = out.rearrange("o (t p) d -> p (o t) d", p=P)
            for t in range(TT):
                for c in range(2):
                    sl = slice(c * 512, (c + 1) * 512)
                    sp.wait_ge(s["final_ready"], 2 * t + c + 1)
                    sp.dma_start(y_rows[:, t, sl], mo[:, t, sl]).then_inc(s["stored"], 16)
            sp.wait_ge(s["stored"], 16 * 2 * TT)

        @block.scalar
        def _(act):
            last = [None]
            n_steps = [0]
            next_unit = [0]

            def did(ins, semaphore=None, value=None):
                if semaphore is None:
                    n_steps[0] += 1
                    semaphore, value = act_step, n_steps[0]
                ins.then_inc(semaphore, 1)
                last[0] = (semaphore, value)

            def settle():
                act.wait_ge(*last[0])

            def high_until(u_end):
                while next_unit[0] <= min(u_end, len(UNITS) - 1):
                    u = next_unit[0]
                    w = UNITS[u][2]
                    act.wait_ge(raw_loaded[u % RAW], 16 * (u // RAW + 1))
                    if u >= SPLIT:
                        wait_unit_used(act, u - SPLIT)
                    did(act.activation(wh[:, u % SPLIT, 0:2 * w], raw[:, u % RAW, 0:2 * w], ACT.Copy), high_done, u + 1)
                    next_unit[0] += 1

            act.dma_start(eye[:], eye_in).then_inc(eye_loaded, 16)
            act.wait_ge(half_set, 1)
            did(act.activation(stat(ZERO), stat(HALF), ACT.Exp))
            act.dma_start(hot, hot_in).then_inc(rel_loaded, 16)
            act.dma_start(rel[0:BUCKETS, :], rel_in).then_inc(rel_loaded, 16)
            for t in range(TT):
                for j in range(2):
                    after_job(act, f"hT{t}{j}")
                    did(act.activation(half_kt(hTh, t, j), heads(tmp[:, j]), ACT.Copy), s["hT_high"], 2 * t + j + 1)
                    if (t, j) == (0, 0):
                        high_until(0)
                high_until(1 + t)
            high_until(3)
            act.dma_start(prob[:, 0:len(LEVELS) * P // 2], levels_in).then_inc(lvl_loaded, 16)
            act.dma_start(hgn[:], hg_norm.to_broadcast([P, P])).then_inc(hgn_loaded, 16)
            act.dma_start(post[:], post_mix.to_broadcast([P, D])).then_inc(post_loaded, 16)
            act.wait_ge(hT1_ready, 2)
            for t in range(TT):
                act.wait_ge(x_loaded[t], 16)
                for c in range(2):
                    if t or c:
                        settle()
                    did(act.activation(relu[:, c], x0[:, t, c * 512:(c + 1) * 512], ACT.Square,
                                       accum_out=stat(OUT_P + 2 * t + c)), s["x_squares"], 2 * t + c + 1)
            act.wait_ge(s["lb_delta"], 1)
            did(act.activation(stat(ONE, H), stat(ONE, H), ACT.Exp), s["one_exp"], 1)
            high_until(7)

            def stage_copy(name, slot, w, src_units):
                high_until(src_units)
                act.wait_ge(s["x_rstd"], 1)
                for t in range(TT):
                    ps = wait_block(act, name, t)
                    did(act.activation(stage[:, slot, t, 0:w], ps[:, 0:w], ACT.Copy, scale=stat(X_RS + t)), *block_read(name, t))

            stage_copy("lat", 0, 512, LAST_UNIT["lat"] + 4)
            for t in range(TT):
                settle()
                did(act.activation(relu[:, 0, 0:RK], stage[:, 0, t, 0:RK], ACT.Square, accum_out=stat(LAT_SS + t)), s["lat_squares"], t + 1)
            stage_copy("idx", 1, 328, LAST_UNIT["idx"] + 4)

            def copy_jobs(jobs, dst):
                for i, name in enumerate(jobs):
                    ps = wait_job(act, name)
                    did(act.activation(dst(i), ps[:, 0:512], ACT.Copy), *job_read(name))

            def flat(ap, i):
                return ap[:, 2 * i:2 * i + 2, :].rearrange("p h t -> p (h t)")

            high_until(12)
            after_job(act, "ckvT")
            did(act.activation(ckvh, ckvT[:], ACT.Copy), s["ckv_high"], 1)
            high_until(13)
            copy_jobs(["iqT0"], lambda i: flat(iqT, 0))
            high_until(15)
            copy_jobs(["iqT1"], lambda i: flat(iqT, 1))
            stage_copy("dq", 2, 512, 17)
            copy_jobs(["kc0", "kc1"], lambda i: flat(kcT, i))
            high_until(18)
            copy_jobs(["vc0", "vc1"], lambda i: vc[:, i, :])
            for i in range(6):
                high_until(19 + i // 2)
                ps = wait_job(act, f"ix{i}")
                if i >= 2:
                    act.wait_ge(s["relu_used"], i - 1)
                did(act.activation(relu[:, i % 2], ps[:, 0:512], ACT.Relu, scale=DI ** -0.5), *job_read(f"ix{i}"))
            stage_copy("hf", 0, 512, 21)
            high_until(22)
            copy_jobs(["dqT0", "dqT1"], lambda i: flat(qT, i))
            high_until(24)
            for i in range(2):
                ps = wait_job(act, f"hfT{i}")
                did(act.activation(flat(pre, i), ps[:, 0:512], ACT.Sigmoid))
                did(act.activation(flat(kT, i), ps[:, 0:512], ACT.Sigmoid, scale=-1.0), *job_read(f"hfT{i}"))
            wait_job(act, "ikT")
            stage_copy("hq", 1, 512, 25)
            high_until(27)
            copy_jobs(["hqT0", "hqT1"], lambda i: flat(hqT, i))
            high_until(29)

            def exps(k):
                act.wait_ge(s["logits_max"], k + 1)
                for t in range(TT):
                    for h in range(H):
                        i = 8 * k + t * H + h
                        row = prob3[:, h, 0:P] if t == 0 else prob3[:, h, P:TW]
                        ins = act.activation(row, row, ACT.Exp, bias=stat(NMAX + i), accum_out=stat(SUM + i))
                        if t == TT - 1 and h == H - 1:
                            did(ins, s["exp_done"], k + 1)
                        else:
                            did(ins)

            def probT_copy(jobs):
                for i, name in enumerate(jobs):
                    ps = wait_job(act, name)
                    did(act.activation(probT[:, 512 * i:512 * (i + 1)], ps[:, 0:512], ACT.Copy), *job_read(name))

            def y_high(jobs, b, k):
                for i, name in enumerate(jobs):
                    ps = wait_job(act, name)
                    did(act.activation(flat(yh[b], i), ps[:, 0:512], ACT.Copy), s["y_high"], 2 * k + i + 1)

            def tokens(name, dst, units):
                high_until(units)
                for t in range(TT):
                    ps = wait_block(act, name, t)
                    did(act.activation(dst[:, t, :], ps[:, 0:512], ACT.Copy, scale=stat(X_RS + t)), *block_read(name, t))

            exps(0)
            tokens("hi", hv, LAST_UNIT["hi"] + 4)
            high_until(33)
            probT_copy(["dP0", "dP1", "dP2"])
            stage_copy("mq", 2, 512, LAST_UNIT["mq"] + 4)
            high_until(35)
            y_high(["dO0", "dO1"], 2, 0)
            copy_jobs(["mqT0", "mqT1"], lambda i: flat(qT, i))
            stage_copy("mk", 0, 512, LAST_UNIT["mk"] + 4)
            high_until(38)
            copy_jobs(["mkT0", "mkT1"], lambda i: flat(kcT, i))
            tokens("mv", mv, LAST_UNIT["mv"] + 4)
            high_until(42)
            exps(1)
            high_until(45)
            for t in range(TT):
                ps = wait_block(act, "hg", t)
                did(act.activation(gw[:, t, :], ps[:, 0:512], ACT.Sigmoid, scale=stat(X_RS + t)), s["hg_sig"], t + 1)
            probT_copy(["mP0", "mP1", "mP2"])
            high_until(47)
            for t in range(TT):
                ps = wait_job(act, f"ho{t}")
                did(act.activation(relu[:, t], ps[:, 0:512], ACT.Square), s["o_squares"], t + 1)
            high_until(48)
            y_high(["mO0", "mO1"], 1, 1)

            def gates(i, c):
                b = BRANCHES[i]
                name = f"gate{b}{c}"
                high_until(LAST_UNIT[name] + 4)
                if c:
                    after_block(act, f"branch{b}0")
                for t in range(TT):
                    ps = wait_block(act, name, t)
                    did(act.activation(sig[:, b, t], ps[:, 0:512], ACT.Sigmoid, scale=stat(X_RS + t)), *block_read(name, t))

            gates(0, 0)
            gates(1, 0)
            y_high(["yaT0", "yaT1"], 0, 2)
            gates(2, 0)
            high_until(FIRST_UNIT[f"gate{BRANCHES[0]}1"] + 5)
            for j in range(2):
                ps = wait_job(act, f"mT{j}")
                did(act.activation(flat(mTh, j), ps[:, 0:512], ACT.Copy), s["mT_high"], j + 1)
            gates(0, 1)
            gates(1, 1)
            gates(2, 1)
            high_until(LAST_UNIT["branch01"] + 6)
            for j in range(2, 4):
                ps = wait_job(act, f"mT{j}")
                did(act.activation(flat(mTh, j), ps[:, 0:512], ACT.Copy), s["mT_high"], j + 1)
            def out_squares(t, c):
                ps = wait_block(act, f"out{c}", t)
                settle()
                did(act.activation(tmp[:, c], ps[:, 0:512], ACT.Square, scale=ROOT, accum_out=stat(OUT_P + 2 * t + c)), s["out_squares"], 2 * t + c + 1)

            def h2_high(t):
                for j in range(2):
                    ps = wait_job(act, f"h2T{t}{j}")
                    did(act.activation(half_kt(hTh, t, j), heads(ps[:]), ACT.Copy), s["h2_high"], 2 * t + j + 1)

            high_until(FIRST_UNIT["fg0"] + 1)
            out_squares(0, 0)
            out_squares(0, 1)
            out_squares(1, 0)
            h2_high(0)
            high_until(FIRST_UNIT["fg0"] + 3)
            out_squares(1, 1)
            h2_high(1)
            high_until(FIRST_UNIT["fg0"] + 5)
            for t in range(TT):
                settle()
                act.wait_ge(s["x1_ready"], TT)
                did(act.activation(mo[:, t, :], x1[:, t, :], ACT.Square, accum_out=stat(X1_SS + t)), s["x1_squares"], t + 1)

            def silu(name, j, w):
                act.wait_ge(s["h2_rstd"], 1)
                if j >= 2:
                    after_block(act, f"fu{j - 2}")
                for t in range(TT):
                    ps = wait_block(act, name, t)
                    ins = act.activation(fg[:, j % 2, t, 0:w], ps[:, 0:w], ACT.Silu, scale=stat(X1_RS + t))
                    if w == 512:
                        did(ins, *block_read(name, t))
                    else:
                        did(ins, s["silu_last"], t + 1)

            def f_high(j, n):
                for i in range(2 * j, 2 * j + n):
                    ps = wait_job(act, f"fT{i}")
                    did(act.activation(fT_h[:, 2 * i:2 * i + 2, :].rearrange("p k t -> p (k t)"), ps[:, 0:512], ACT.Copy),
                        s["fT_high"], i + 1)

            for j in range(5):
                if j:
                    high_until(LAST_UNIT[f"fu{j - 1}"] + 6)
                    f_high(j - 1, 2)
                high_until(LAST_UNIT[f"fg{j}"] + 4)
                silu(f"fg{j}", j, 512)
            high_until(LAST_UNIT["fu4"] + 6)
            f_high(4, 2)
            high_until(LAST_UNIT["fgu"] + 4)
            silu("fgu", 5, 256)
            high_until(LAST_UNIT["fgu"] + 7)
            f_high(5, 1)
            for c in range(2):
                high_until(LAST_UNIT[f"down{c}"] + 4)
                for t in range(TT):
                    ps = wait_block(act, f"down{c}", t)
                    settle()
                    did(act.activation(tmp[:, t], ps[:, 0:512], ACT.Square, scale=ROOT, accum_out=stat(DN_P + 2 * t + c)),
                        s["down_squares"], 2 * c + t + 1)

        @block.vector
        def _(dve):
            last = [None]
            n_steps = [0]
            next_unit = [0]

            def did(ins, semaphore=None, value=None):
                if semaphore is None:
                    n_steps[0] += 1
                    semaphore, value = dve_step, n_steps[0]
                ins.then_inc(semaphore, 1)
                last[0] = (semaphore, value)

            def settle():
                if last[0] is not None:
                    dve.wait_ge(*last[0])

            def low_until(u_end):
                while next_unit[0] <= min(u_end, len(UNITS) - 1):
                    u = next_unit[0]
                    w = UNITS[u][2]
                    dve.wait_ge(high_done, u + 1)
                    did(dve.tensor_tensor(wl[:, u % SPLIT, 0:2 * w], raw[:, u % RAW, 0:2 * w],
                                          wh[:, u % SPLIT, 0:2 * w].bitcast(F32), ALU.subtract), low_done, u + 1)
                    next_unit[0] += 1

            def flat(ap, i):
                return ap[:, 2 * i:2 * i + 2, :].rearrange("p h t -> p (h t)")

            dve.wait_ge(cols_loaded, 16)
            a, b_ = COLS["lb"]
            did(dve.tensor_tensor(stat(ONE, H), cols[:, a:b_], cols[:, a:b_], ALU.subtract), s["lb_delta"], 1)

            def scale_input(t, j):
                ps = wait_job(dve, f"hT{t}{j}")
                w4 = cols[:, 4 * j:4 * j + 4].rearrange("p (k o) -> p k o", o=1).to_broadcast([P, 4, P])
                settle()
                did(dve.tensor_tensor(heads(tmp[:, j]), heads(ps[:]), w4, ALU.mult), *job_read(f"hT{t}{j}"))

            def low_input(j):
                dve.wait_ge(s["hT_high"], j + 1)
                did(dve.tensor_tensor(half_kt(hTl, 0, j), heads(tmp[:, j]), half_kt(hTh, 0, j).bitcast(F32), ALU.subtract),
                    s["hT_ready"], j + 1)

            scale_input(0, 0)
            scale_input(0, 1)
            low_input(0)
            low_until(0)
            low_input(1)
            scale_input(1, 0)
            low_until(1)
            scale_input(1, 1)
            low_until(4)
            dve.wait_ge(s["x_squares"], 4)
            parts = stat(OUT_P, 4).rearrange("p (t c) -> p t c", c=2)
            did(dve.tensor_tensor(stat(X_SS, 2), parts[:, :, 0], parts[:, :, 1], ALU.add), s["out_sums"], 1)
            low_until(5)
            dve.wait_ge(s["one_exp"], 1)
            did(dve.reciprocal(stat(OML, H), stat(ONE, H)))
            settle()
            did(dve.tensor_tensor(stat(OML, H), stat(OML, H), stat(ONE, H), ALU.mult))
            settle()
            did(dve.tensor_tensor(stat(LB, H), stat(OML, H), stat(OML, H), ALU.subtract))
            settle()
            did(dve.tensor_scalar(stat(OML, H), stat(LB, H), -1.0, 1.0, ALU.mult, ALU.add))
            low_until(6)
            ps = wait_job(dve, "rel")
            did(dve.tensor_copy(rel8, ps[0:2 * H, 0:TW]), *job_read("rel"))
            low_until(9)

            dve.wait_ge(s["lat_rstd"], 1)
            for t in range(TT):
                did(dve.tensor_scalar(stage[:, 0, t, 0:RK], stage[:, 0, t, 0:RK], stat(LAT_RS + t), None, ALU.mult),
                    s["ckv_ready"], t + 1)
            low_until(11)
            ps = wait_job(dve, "ckvT")
            a = COLS["kv_norm"][0]
            did(dve.tensor_tensor(ckvT[:], heads(ps[:], RT), cols[:, a:a + RT].rearrange("p (k o) -> p k o", o=1).to_broadcast([P, RT, S]), ALU.mult),
                *job_read("ckvT"))
            low_until(12)
            dve.wait_ge(s["ckv_high"], 1)
            did(dve.tensor_tensor(ckvl, ckvT[:], ckvh.bitcast(F32), ALU.subtract), s["ckv_low"], 1)
            after_block(dve, "idx")
            ik = stage[:, 1, :, 256:256 + DI]
            did(dve.tensor_reduce(stat(IK_MEAN, 2), ik, AX.X, ALU.add))
            settle()
            did(dve.tensor_scalar(stat(IK_MEAN, 2), stat(IK_MEAN, 2), -1.0 / DI, None, ALU.mult))
            settle()
            for t in range(TT):
                did(dve.tensor_scalar(ikc[:, t], stage[:, 1, t, 256:256 + DI], stat(IK_MEAN + t), None, ALU.add))
            did(dve.tensor_scalar(iws[:], stage[:, 1, :, 256 + DI:256 + DI + NI], NI ** -0.5, None, ALU.mult))
            settle()
            did(dve.tensor_tensor(ikn[:, :, 0:DI], ikc[:], ikc[:], ALU.mult))
            settle()
            did(dve.tensor_reduce(stat(IK_SS, 2), ikn[:, :, 0:DI], AX.X, ALU.add), s["ik_squares"], 1)
            low_until(13)
            dve.wait_ge(s["ik_rstd"], 1)
            settle()
            for t in range(TT):
                for c in range(2):
                    did(dve.tensor_scalar(ikn[:, t, c * DI:(c + 1) * DI], ikc[:, t], stat(IK_RS + t), None, ALU.mult),
                        s["ik_ready"], 2 * t + c + 1)
            low_until(16)
            ps = wait_job(dve, "ikT")
            did(dve.tensor_scalar(ikT[:], ps[:, 0:S], col("ik_w"), col("ik_b"), ALU.mult, ALU.add), *job_read("ikT"))
            low_until(19)
            dve.wait_ge(lvl_loaded, 16)
            did(dve.tensor_copy(lvl[:], prob[:, 0:len(LEVELS) * P // 2]))

            def add_heads(i):
                after_job(dve, f"ix{i}")
                t, its_heads = INDEXER[i]
                w = 512 // len(its_heads)
                row = score[:, 0:P] if t == 0 else score[:, P:TW]
                for k, h in enumerate(its_heads):
                    part = relu[:, i % 2, k * w:(k + 1) * w]
                    settle()
                    if h == 0:
                        ins = dve.tensor_scalar(row, part, iws[:, t, h:h + 1], None, ALU.mult)
                    else:
                        ins = dve.scalar_tensor_tensor(out=row, in0=part, scalar=iws[:, t, h:h + 1], in1=row, op0=ALU.mult, op1=ALU.add)
                    if k == len(its_heads) - 1:
                        did(ins, s["relu_used"], i + 1)
                    else:
                        did(ins)

            for i in range(6):
                add_heads(i)
                if i % 2:
                    low_until(20 + i // 2)

            def diagonal():
                eye_h = eye[:].rearrange("p (o k) -> p o k", o=1).to_broadcast([P, H, P])
                for t in range(TT):
                    ps = wait_job(dve, f"diag{t}")
                    did(dve.tensor_tensor(tri3[:, :, 2 * P * t:2 * P * t + P], heads(ps[:]), eye_h, ALU.mult), *job_read(f"diag{t}"))

            dve.wait_ge(s["score_ready"], 2)
            for r in range(NKEEP // 8):
                src = score if r == 0 else work
                for t, (a, z) in enumerate(((0, P), (P, TW))):
                    if r:
                        settle()
                    did(dve.max(top8[:, t], src[:, a:z]))
                    settle()
                    did(dve.match_replace(work[:, a:z], top8[:, t], src[:, a:z], TAKEN))
                if r in (1, 2, 4, 5):
                    low_until(22 + r)
                if r == 6:
                    low_until(27)
                    diagonal()
                if r == 3:
                    after_job(dve, "hfT1")
                    for h in range(H):
                        did(dve.tensor_scalar(kT[:, h], kT[:, h], stat(OML + h), None, ALU.mult))
                        did(dve.tensor_scalar(pre[:, h], pre[:, h], stat(OML + h), stat(LB + h), ALU.mult, ALU.add))
                    settle()
                    did(dve.tensor_scalar(pre[:], pre[:], TINY, None, ALU.max), s["gates_ready"], 1)
            settle()
            did(dve.tensor_tensor(work[:], work[:], score[:], ALU.is_equal))

            def logits(pre_, k, head0):
                for i in range(3):
                    ps = wait_job(dve, f"{pre_}l{i}")
                    if i == 0:
                        bs = bias[:, head0:head0 + H, P:S]
                        dst = prob3[:, :, 0:P]
                        src = heads(ps[:])
                    else:
                        hh = 2 * (i - 1)
                        bs = bias[:, head0 + hh:head0 + hh + 2, :]
                        dst = prob3[:, hh:hh + 2, P:TW]
                        src = heads(ps[:], 2)
                    did(dve.scalar_tensor_tensor(out=dst, in0=src, scalar=SCALE, in1=bs, op0=ALU.mult, op1=ALU.add), *job_read(f"{pre_}l{i}"))

            def maxima(k):
                settle()
                did(dve.tensor_reduce(stat(NMAX + 8 * k, H), prob3[:, :, 0:P], AX.X, ALU.max, negate=True))
                did(dve.tensor_reduce(stat(NMAX + 8 * k + H, H), prob3[:, :, P:TW], AX.X, ALU.max, negate=True), s["logits_max"], k + 1)

            def normalise(k):
                dve.wait_ge(s["exp_done"], k + 1)
                did(dve.reciprocal(stat(RCP + 8 * k, 8), stat(SUM + 8 * k, 8)))
                settle()
                for t in range(TT):
                    for h in range(H):
                        row = prob3[:, h, 0:P] if t == 0 else prob3[:, h, P:TW]
                        ins = dve.tensor_scalar(row, row, stat(RCP + 8 * k + t * H + h), None, ALU.mult)
                        if t == TT - 1 and h == H - 1:
                            did(ins, s["prob_ready"], k + 1)
                        else:
                            did(ins)

            dve.wait_ge(bias_loaded, 16 * P // SKEW)
            logits("d", 0, H)
            low_until(28)
            settle()
            for t in range(TT):
                a, z = (0, P) if t == 0 else (P, TW)
                keep = work[:, a:z].rearrange("p (o k) -> p o k", o=1).to_broadcast([P, H, z - a])
                did(dve.scalar_tensor_tensor(out=prob3[:, :, a:z], in0=keep, scalar=NEG, in1=prob3[:, :, a:z], op0=ALU.mult, op1=ALU.add))
            maxima(0)
            low_until(29)

            def level(i):
                settle()
                w = LEVELS[i]
                g = P // (2 * w)
                mask = lvl3[:, i, :].rearrange("p (o g k) -> p o g k", o=1, k=w).to_broadcast([P, H, g, w])
                ps = wait_job(dve, f"L{w}")
                for t in range(TT):
                    upper = tri3[:, :, 2 * P * t:2 * P * t + P].rearrange("p h (g two k) -> p h g two k", two=2, k=w)[:, :, :, 1, :]
                    src = ps[:, t * S:(t + 1) * S].rearrange("p (h g k) -> p h g k", h=H, k=w)
                    ins = dve.copy_predicated(upper, mask, src)
                    if t == TT - 1:
                        did(ins, *job_read(f"L{w}"))
                    else:
                        did(ins)

            def y_low(jobs, b, k):
                for i, name in enumerate(jobs):
                    ps = wait_job(dve, name)
                    dve.wait_ge(s["y_high"], 2 * k + i + 1)
                    did(dve.tensor_tensor(flat(yl[b], i), ps[:, 0:512], flat(yh[b], i).bitcast(F32), ALU.subtract), *job_read(name))

            level(0)
            low_until(31)
            level(1)
            normalise(0)
            low_until(32)
            level(2)
            low_until(34)
            level(3)
            low_until(35)
            y_low(["dO0", "dO1"], 2, 0)
            low_until(36)
            level(4)
            low_until(37)
            level(5)
            low_until(39)
            logits("m", 1, 0)
            maxima(1)
            low_until(40)
            level(6)
            low_until(42)
            ps = wait_job(dve, "L128")
            did(dve.tensor_copy(tri3[:, :, P:2 * P], heads(ps[:])), *job_read("L128"))
            low_until(44)
            normalise(1)
            low_until(45)
            dve.wait_ge(hgn_loaded, 16)
            for t in range(TT):
                ps = wait_block(dve, "hg", t)
                dve.wait_ge(s["hg_sig"], t + 1)
                settle()
                did(dve.scalar_tensor_tensor(out=gw[:, t], in0=ps[:, 0:512], scalar=stat(X_RS + t), in1=gw[:, t], op0=ALU.mult, op1=ALU.mult),
                    *block_read("hg", t))
            for t in range(TT):
                settle()
                hgn_h = hgn[:].rearrange("p (o k) -> p o k", o=1).to_broadcast([P, H, P])
                did(dve.tensor_tensor(heads(gw[:, t]), heads(gw[:, t]), hgn_h, ALU.mult))
            low_until(47)
            for t in range(TT):
                dve.wait_ge(s["o_squares"], t + 1)
                did(dve.tensor_reduce(stat(O_SS + H * t, H), heads(relu[:, t]), AX.X, ALU.add), s["o_sums"], t + 1)
            low_until(48)
            dve.wait_ge(s["o_rstd"], 1)
            for t in range(TT):
                ps = wait_job(dve, f"ho{t}")
                for h in range(H):
                    settle()
                    ins = dve.scalar_tensor_tensor(out=stage[:, 1, t, h * P:(h + 1) * P], in0=ps[:, h * P:(h + 1) * P],
                                                   scalar=stat(O_RS + H * t + h), in1=gw[:, t, h * P:(h + 1) * P], op0=ALU.mult, op1=ALU.mult)
                    if h == H - 1:
                        did(ins, *job_read(f"ho{t}"))
                    else:
                        did(ins)
            low_until(49)
            y_low(["mO0", "mO1"], 1, 1)
            low_until(53)
            y_low(["yaT0", "yaT1"], 0, 2)

            n_merged = [0]

            def merge(c):
                for i, b in enumerate(BRANCHES):
                    low_until(LAST_UNIT[f"branch{b}{c}"] + 3)
                    after_block(dve, f"gate{b}{c}")
                    for t in range(TT):
                        ps = wait_block(dve, f"branch{b}{c}", t)
                        dst = merged[:, t, c * 512:(c + 1) * 512]
                        out_ = dst if i == 0 else tmp[:, t]
                        settle()
                        did(dve.tensor_tensor(out_, ps[:, 0:512], sig[:, b, t], ALU.mult), *block_read(f"branch{b}{c}", t))
                    settle()
                    if i:
                        for t in range(TT):
                            dst = merged[:, t, c * 512:(c + 1) * 512]
                            n_merged[0] += 1
                            did(dve.tensor_tensor(dst, dst, tmp[:, t], ALU.add), s["merged"], n_merged[0])
                    if (c, i) == (1, 0):
                        dve.wait_ge(x1_loaded, 32)
                        dve.wait_ge(post_loaded, 16)
                        did(dve.tensor_tensor(pw, wf, post[:], ALU.mult))
                        low_until(LAST_UNIT["branch11"] + 4)
                        for t in range(TT):
                            did(dve.tensor_tensor(h2[:, t], x1[:, t], wf, ALU.mult))

            def m_low(j):
                ps = wait_job(dve, f"mT{j}")
                dve.wait_ge(s["mT_high"], j + 1)
                did(dve.tensor_tensor(flat(mTl, j), ps[:, 0:512], flat(mTh, j).bitcast(F32), ALU.subtract), *job_read(f"mT{j}"))

            merge(0)
            low_until(FIRST_UNIT[f"gate{BRANCHES[0]}1"] + 4)
            m_low(0)
            m_low(1)
            merge(1)
            low_until(LAST_UNIT["branch01"] + 5)
            m_low(2)
            m_low(3)
            def weigh(t, c):
                sl = slice(c * 512, (c + 1) * 512)
                ps = wait_block(dve, f"out{c}", t)
                dve.wait_ge(s["out_squares"], 2 * t + c + 1)
                did(dve.tensor_tensor(mow[:, t, sl], ps[:], pw[:, sl], ALU.mult))
                if c == 0:
                    did(dve.tensor_tensor(mo[:, t, sl], ps[:], post[:, sl], ALU.mult), *block_read(f"out{c}", t))

            def second_input(t):
                dve.wait_ge(s["out_squares"], 2 * t + 2)
                did(dve.scalar_tensor_tensor(out=stat(OUT_SS + t), in0=stat(OUT_P + 2 * t), scalar=EPS, in1=stat(OUT_P + 2 * t + 1),
                                             op0=ALU.add, op1=ALU.add), s["out_mean"], t + 1)
                weigh(t, 1)
                dve.wait_ge(s["out_rstd"], t + 1)
                settle()
                for c in range(2):
                    sl = slice(c * 512, (c + 1) * 512)
                    did(dve.scalar_tensor_tensor(out=h2[:, t, sl], in0=mow[:, t, sl], scalar=stat(OUT_RS + t), in1=h2[:, t, sl],
                                                 op0=ALU.mult, op1=ALU.add), s["h2_input"], 2 * t + c + 1)

            def h2_low(t):
                for j in range(2):
                    ps = wait_job(dve, f"h2T{t}{j}")
                    dve.wait_ge(s["h2_high"], 2 * t + j + 1)
                    did(dve.tensor_tensor(half_kt(hTl, t, j), heads(ps[:]), half_kt(hTh, t, j).bitcast(F32), ALU.subtract),
                        *job_read(f"h2T{t}{j}"))

            low_until(FIRST_UNIT["fg0"] + 1)
            weigh(0, 0)
            second_input(0)
            h2_low(0)
            weigh(1, 0)
            low_until(FIRST_UNIT["fg0"] + 3)
            second_input(1)
            h2_low(1)
            for t in range(TT):
                did(dve.tensor_tensor(mo[:, t, 512:D], wait_block(dve, "out1", t)[:], post[:, 512:D], ALU.mult), *block_read("out1", t))
            low_until(FIRST_UNIT["fg0"] + 5)
            for t in range(TT):
                settle()
                did(dve.scalar_tensor_tensor(out=x1[:, t], in0=mo[:, t], scalar=stat(OUT_RS + t), in1=x1[:, t],
                                             op0=ALU.mult, op1=ALU.add), s["x1_ready"], t + 1)

            def up(name, j, w, off):
                if j < 5:
                    after_block(dve, f"fg{j}")
                else:
                    dve.wait_ge(s["silu_last"], 2)
                if j >= 2:
                    wait_job(dve, f"fT{2 * (j - 2) + 1}")
                for t in range(TT):
                    ps = wait_block(dve, name, t)
                    settle()
                    did(dve.scalar_tensor_tensor(out=fa[:, j % 2, t, 0:w], in0=ps[:, off:off + w], scalar=stat(X1_RS + t),
                                                 in1=fg[:, j % 2, t, 0:w], op0=ALU.mult, op1=ALU.mult), *block_read(name, t))

            def f_low(j, n):
                for i in range(2 * j, 2 * j + n):
                    ps = wait_job(dve, f"fT{i}")
                    dve.wait_ge(s["fT_high"], i + 1)
                    did(dve.tensor_tensor(fT_l[:, 2 * i:2 * i + 2, :].rearrange("p k t -> p (k t)"), ps[:, 0:512],
                                          fT_h[:, 2 * i:2 * i + 2, :].rearrange("p k t -> p (k t)").bitcast(F32), ALU.subtract),
                        *job_read(f"fT{i}"))

            for j in range(5):
                if j:
                    low_until(LAST_UNIT[f"fu{j - 1}"] + 6)
                    f_low(j - 1, 2)
                low_until(LAST_UNIT[f"fu{j}"] + 4)
                up(f"fu{j}", j, 512, 0)
            low_until(LAST_UNIT["fu4"] + 6)
            f_low(4, 2)
            low_until(LAST_UNIT["fgu"] + 4)
            up("fgu", 5, 256, 256)
            low_until(LAST_UNIT["fgu"] + 7)
            f_low(5, 1)
            low_until(len(UNITS))
            dve.wait_ge(post_loaded, 32)
            for c in range(2):
                for t in range(TT):
                    sl = slice(c * 512, (c + 1) * 512)
                    ps = wait_block(dve, f"down{c}", t)
                    if c:
                        dve.wait_ge(s["down_squares"], TT + t + 1)
                        settle()
                        did(dve.scalar_tensor_tensor(out=stat(DN_SS + t), in0=stat(DN_P + 2 * t), scalar=EPS, in1=stat(DN_P + 2 * t + 1),
                                                     op0=ALU.add, op1=ALU.add), s["down_mean"], t + 1)
                    else:
                        dve.wait_ge(s["x1_squares"], TT)
                    did(dve.tensor_tensor(mo[:, t, sl], ps[:], post[:, sl], ALU.mult))
                    if c:
                        dve.wait_ge(s["down_rstd"], t + 1)
                        settle()
                        for k in range(2):
                            sk = slice(k * 512, (k + 1) * 512)
                            did(dve.scalar_tensor_tensor(out=mo[:, t, sk], in0=mo[:, t, sk], scalar=stat(DN_RS + t), in1=x1[:, t, sk],
                                                         op0=ALU.mult, op1=ALU.add), s["final_ready"], 2 * t + k + 1)

        @block.gpsimd
        def _(pool):
            last = [None]
            n_steps = [0]

            def did(ins, semaphore=None, value=None):
                if semaphore is None:
                    n_steps[0] += 1
                    semaphore, value = pool_step, n_steps[0]
                ins.then_inc(semaphore, 1)
                last[0] = (semaphore, value)

            def settle():
                pool.wait_ge(*last[0])

            did(pool.memset(rel[BUCKETS:BUCKETS + 1, :], NEG), rel_row, 1)
            settle()
            did(pool.memset(stat(HALF, 8), -0.5), half_set, 1)
            for j in range(2):
                pool.wait_ge(s["hT_high"], 2 + j + 1)
                did(pool.tensor_tensor(half_kt(hTl, 1, j), heads(tmp[:, j]), half_kt(hTh, 1, j).bitcast(F32), ALU.subtract),
                    hT1_ready, j + 1)
            did(pool.memset(suf[:], 1.0))

            def rstd(dst, src, n, count, done, value=1):
                settle()
                did(pool.tensor_scalar(stat(RMS_TMP, n), stat(src, n), 1.0 / count, EPS, ALU.mult, ALU.add))
                settle()
                did(pool.tensor_tensor(stat(dst, n), stat(RMS_TMP, n), stat(HALF, n), ALU.pow), done, value)

            pool.wait_ge(s["out_sums"], 1)
            rstd(X_RS, X_SS, 2, D, s["x_rstd"])
            pool.wait_ge(s["lat_squares"], 2)
            rstd(LAT_RS, LAT_SS, 2, RK, s["lat_rstd"])
            pool.wait_ge(s["ik_squares"], 1)
            rstd(IK_RS, IK_SS, 2, DI, s["ik_rstd"])
            for t in range(TT):
                pool.wait_ge(s["relu_used"], 2 if t == 0 else 6)
                diag = score[:, 0:P] if t == 0 else score[:, 2 * P:TW]
                did(pool.affine_select(out=diag, in_=diag, compare_op=ALU.is_ge, fill=NEG, base=0,
                                       pattern=[[-1, P]], channel_multiplier=1), s["score_ready"], t + 1)

            pool.wait_ge(s["gates_ready"], 1)
            after_job(pool, "hqT1")

            def halves(ap, w):
                v = ap.rearrange("p h t -> p (h t)").rearrange("p (g two s) -> p g two s", two=2, s=w)
                return v[:, :, 0, :], v[:, :, 1, :]

            for i, w in enumerate(LEVELS + [P]):
                g = H * S // (2 * w)
                a_lo, a_up = halves(att[i % 2], w)
                k_lo, _ = halves(kT[:], w)
                _, q_up = halves(hqT[:], w)
                p_lo, p_up = halves(pre[:], w)
                s_lo, s_up = halves(suf[:], w)
                if i >= 2:
                    wait_job(pool, f"L{LEVELS[i - 2]}")
                did(pool.tensor_tensor(a_lo, k_lo, s_lo, ALU.mult))
                did(pool.tensor_tensor(a_up, q_up, p_up, ALU.mult), s["level_built"], i + 1)
                settle()
                if w < P:
                    did(pool.tensor_tensor(s_lo, s_lo, p_up[:, :, w - 1:w].to_broadcast([P, g, w]), ALU.mult))
                    settle()
                    did(pool.tensor_tensor(p_up, p_up, p_lo[:, :, w - 1:w].to_broadcast([P, g, w]), ALU.mult))
                    settle()
            pool.wait_ge(s["o_sums"], 2)
            rstd(O_RS, O_SS, 8, P, s["o_rstd"])

            def root(dst, src, done, value):
                did(pool.tensor_tensor(stat(dst), stat(src), stat(HALF), ALU.pow), done, value)

            for t in range(TT):
                pool.wait_ge(s["out_mean"], t + 1)
                root(OUT_RS + t, OUT_SS + t, s["out_rstd"], t + 1)
            pool.wait_ge(s["x1_squares"], 2)
            rstd(X1_RS, X1_SS, 2, D, s["h2_rstd"])
            for t in range(TT):
                pool.wait_ge(s["down_mean"], t + 1)
                root(DN_RS + t, DN_SS + t, s["down_rstd"], t + 1)

        @block.tensor
        def _(pe):
            next_unit = [0]
            next_job = [0]

            def begin(name):
                assert JOBS[next_job[0]] == name, (JOBS[next_job[0]], name)
                next_job[0] += 1
                b, n = job_bank(name)
                if n:
                    pe.wait_ge(bank_read[b], n)
                return bank[b]

            def end(name, ins):
                ins.then_inc(bank_full[job_bank(name)[0]], 1)

            def lhs_of(name):
                if name.startswith("branch"):
                    b = int(name[6])
                    return yh[b], yl[b]
                if name.startswith("out"):
                    return mTh, mTl
                if name.startswith("down"):
                    return fT_h, fT_l
                return hTh, hTl

            def wait_weights(u):
                pe.wait_ge(low_done, u + 1)

            def products(u, t):
                b, kt0, w = UNITS[u]
                name, n_kt, _ = BLOCKS[b]
                high, low = lhs_of(name)
                if t == 0:
                    wait_weights(u)
                slot = u % SPLIT
                rh = wh[:, slot, 0:2 * w].rearrange("p (k n) -> p k n", k=2)
                rl = wl[:, slot, 0:2 * w].rearrange("p (k n) -> p k n", k=2)
                bk, n = block_bank(name, t)
                if kt0 == 0 and n:
                    pe.wait_ge(bank_read[bk], n)
                for k in range(2):
                    kt = kt0 + k
                    for lhs, rhs in ((high, rh), (high, rl), (low, rh)):
                        first = kt == 0 and lhs is high and rhs is rh
                        final = kt == n_kt - 1 and lhs is low
                        ins = pe.matmul(bank[bk][:, 0:w], lhs[:, kt, t * P:(t + 1) * P], rhs[:, k], start=first, stop=final)
                if kt0 + 2 == n_kt:
                    ins.then_inc(bank_full[bk], 1)
                elif t == TT - 1:
                    ins.then_inc(unit_used, 1)

            def units(u_end):
                while next_unit[0] <= u_end:
                    for t in range(TT):
                        products(next_unit[0], t)
                    next_unit[0] += 1

            def units_by_tile(u_end):
                for t in range(TT):
                    for u in range(next_unit[0], u_end + 1):
                        products(u, t)
                next_unit[0] = u_end + 1

            def transposes(name, sources):
                ps = begin(name)
                for i, src in enumerate(sources):
                    ins = pe.transpose(ps[:, i * P:(i + 1) * P], src, eye[:])
                end(name, ins)

            def tiles(src, h0=None):
                return [src[:, t, (h0 + k) * P:(h0 + k + 1) * P] for k in range(2) for t in range(TT)]

            pe.wait_ge(eye_loaded, 16)
            for t in range(TT):
                pe.wait_ge(x_loaded[t], 16)
                for j in range(2):
                    transposes(f"hT{t}{j}", [x0[:, t, (4 * j + k) * P:(4 * j + k + 1) * P] for k in range(4)])
            for t in range(TT):
                pe.wait_ge(hT1_ready if t else s["hT_ready"], 1)
                products(0, t)
                products(1, t)
            next_unit[0] = 2
            pe.wait_ge(s["hT_ready"], 2)
            pe.wait_ge(hT1_ready, 2)
            units(4)
            pe.wait_ge(rel_loaded, 32)
            pe.wait_ge(rel_row, 1)
            ps = begin("rel")
            end("rel", pe.matmul(ps[0:2 * H, 0:TW], rel[:], hot, start=True, stop=True))
            units(9)
            pe.wait_ge(s["ckv_ready"], 2)
            transposes("ckvT", [stage[:, 0, t, k * P:(k + 1) * P] for k in range(RT) for t in range(TT)])
            transposes("iqT0", tiles(stage[:, 0], 2))
            units(10)
            after_block(pe, "idx")
            transposes("iqT1", tiles(stage[:, 1], 0))
            units(11)
            pe.wait_ge(s["ckv_low"], 1)
            u = next_unit[0]
            wait_weights(u)
            for i in range(2):
                ps = begin(f"kc{i}")
                for k in range(2):
                    h = 2 * i + k
                    for r in range(RT):
                        for w_, c_ in ((wh, ckvh), (wl, ckvh), (wh, ckvl)):
                            at = r * HW + h * P
                            ins = pe.matmul(ps[:, k * S:(k + 1) * S], w_[:, u % SPLIT, at:at + P], c_[:, r, :],
                                            start=r == 0 and w_ is wh and c_ is ckvh, stop=r == RT - 1 and c_ is ckvl)
                end(f"kc{i}", ins)
            u += 1
            wait_weights(u)
            for t in range(TT):
                ps = begin(f"vc{t}")
                for r in range(RT):
                    for c_, w_ in ((ckvh, wh), (ckvh, wl), (ckvl, wh)):
                        ins = pe.matmul(ps[:], c_[:, r, t * P:(t + 1) * P], w_[:, u % SPLIT, r * HW:(r + 1) * HW],
                                        start=r == 0 and w_ is wh and c_ is ckvh, stop=r == RT - 1 and c_ is ckvl)
                end(f"vc{t}", ins)
            next_unit[0] = u + 1
            pe.wait_ge(s["ik_ready"], 4)
            transposes("ikT", [ikn[:, t] for t in range(TT)])
            units(14)
            after_job(pe, "iqT1")
            after_job(pe, "ikT")
            for i in range(6):
                if i % 2 == 0:
                    units(15 + i // 2)
                ps = begin(f"ix{i}")
                t, its_heads = INDEXER[i]
                w = 512 // len(its_heads)
                for k, h in enumerate(its_heads):
                    b = DI * (h % 2)
                    ins = pe.matmul(ps[:, k * w:(k + 1) * w], iqT[b:b + DI, h // 2, t * P:(t + 1) * P], ikT[b:b + DI, 0:w], start=True, stop=True)
                end(f"ix{i}", ins)
            units(18)
            after_block(pe, "dq")
            for i in range(2):
                transposes(f"dqT{i}", tiles(stage[:, 2], 2 * i))
            units(20)
            after_block(pe, "hf")
            for i in range(2):
                transposes(f"hfT{i}", tiles(stage[:, 0], 2 * i))

            def logits(kind):
                for i in range(3):
                    ps = begin(f"{kind}l{i}")
                    for k in range(H if i == 0 else 2):
                        h = k if i == 0 else 2 * (i - 1) + k
                        t, w = (0, P) if i == 0 else (1, S)
                        ins = pe.matmul(ps[:, k * w:(k + 1) * w], qT[:, h, t * P:(t + 1) * P], kcT[:, h, 0:w], start=True, stop=True)
                    end(f"{kind}l{i}", ins)

            def prob_transposes(kind):
                for i in range(3):
                    transposes(f"{kind}P{i}", [prob[:, (4 * i + k) * P:(4 * i + k + 1) * P] for k in range(4)])

            def values(kind, v):
                for i in range(2):
                    ps = begin(f"{kind}O{i}")
                    for k in range(2):
                        h = 2 * i + k
                        pe.matmul(ps[:, k * S:(k + 1) * S], v[:, 0, h * P:(h + 1) * P], probT3[:, h, 0:S], start=True, stop=False)
                        ins = pe.matmul(ps[:, k * S + P:(k + 1) * S], v[:, 1, h * P:(h + 1) * P], probT3[:, h, S:TW], start=False, stop=True)
                    end(f"{kind}O{i}", ins)

            units(23)
            after_block(pe, "hq")
            for i in range(2):
                transposes(f"hqT{i}", tiles(stage[:, 1], 2 * i))
            units(24)
            after_job(pe, "hqT1")
            pe.wait_ge(s["gates_ready"], 1)
            for t in range(TT):
                ps = begin(f"diag{t}")
                for h in range(H):
                    ins = pe.matmul(ps[:, h * P:(h + 1) * P], kT[:, h, t * P:(t + 1) * P], hqT[:, h, t * P:(t + 1) * P], start=True, stop=True)
                end(f"diag{t}", ins)

            def level(i):
                pe.wait_ge(s["level_built"], i + 1)
                w = LEVELS[i]
                ps = begin(f"L{w}")
                for t in range(TT):
                    for h in range(H):
                        a_h = att[i % 2][:, h, t * P:(t + 1) * P]
                        upper = a_h.rearrange("p (g two k) -> p g two k", two=2, k=w)[:, :, 1, :]
                        at = t * S + h * P // 2
                        ins = pe.matmul(ps[:, at:at + P // 2], a_h, upper, start=True, stop=True)
                end(f"L{w}", ins)

            units(25)
            after_job(pe, "dqT1")
            after_job(pe, "kc1")
            logits("d")
            units(26)
            level(0)
            units(28)
            level(1)
            units(29)
            level(2)
            units(30)
            pe.wait_ge(s["prob_ready"], 1)
            prob_transposes("d")
            units(31)
            level(3)
            units(32)
            after_job(pe, "dP2")
            after_job(pe, "vc1")
            values("d", vc)
            after_block(pe, "mq")
            for i in range(2):
                transposes(f"mqT{i}", tiles(stage[:, 2], 2 * i))
            units(33)
            level(4)
            units(34)
            level(5)
            units(35)
            after_block(pe, "mk")
            for i in range(2):
                transposes(f"mkT{i}", tiles(stage[:, 0], 2 * i))
            units(36)
            after_job(pe, "mqT1")
            after_job(pe, "mkT1")
            logits("m")
            units(37)
            level(6)
            units(39)
            pe.wait_ge(s["level_built"], len(LEVELS) + 1)
            ps = begin("L128")
            for h in range(H):
                a_h = att[len(LEVELS) % 2][:, h, :]
                ins = pe.matmul(ps[:, h * P:(h + 1) * P], a_h[:, 0:P], a_h[:, P:S], start=True, stop=True)
            end("L128", ins)
            units(42)
            pe.wait_ge(s["prob_ready"], 2)
            prob_transposes("m")
            units(43)
            after_job(pe, "L128")
            after_block(pe, "hi")
            for t in range(TT):
                ps = begin(f"ho{t}")
                for h in range(H):
                    hs = slice(h * P, (h + 1) * P)
                    if t == 0:
                        ins = pe.matmul(ps[:, hs], tri3[:, h, 0:P], hv[:, 0, hs], start=True, stop=True)
                    else:
                        pe.matmul(ps[:, hs], tri3[:, h, P:2 * P], hv[:, 0, hs], start=True, stop=False)
                        ins = pe.matmul(ps[:, hs], tri3[:, h, 2 * P:TW], hv[:, 1, hs], start=False, stop=True)
                end(f"ho{t}", ins)
            units(44)
            after_job(pe, "mP2")
            after_block(pe, "mv")
            values("m", mv)
            units(49)
            after_job(pe, "ho1")
            for i in range(2):
                transposes(f"yaT{i}", tiles(stage[:, 1], 2 * i))
            for c in range(2):
                if c == 1:
                    units(FIRST_UNIT[f"gate{BRANCHES[0]}1"] + 1)
                    pe.wait_ge(s["merged"], 4)
                    for j in range(2):
                        transposes(f"mT{j}", tiles(merged, 2 * j))
                units(LAST_UNIT[f"gate{BRANCHES[2]}{c}"])
                if c == 0:
                    after_job(pe, "mO1")
                    after_job(pe, "dO1")
                    after_job(pe, "yaT1")
                units(LAST_UNIT[f"branch{BRANCHES[2]}{c}"])
            after_job(pe, "mT1")
            units(FIRST_UNIT["out1"])
            pe.wait_ge(s["merged"], 8)
            for j in range(2, 4):
                transposes(f"mT{j}", tiles(merged, 2 * j))
            units(FIRST_UNIT["out1"] + 1)
            after_job(pe, "mT3")
            def second_input(t):
                for j in range(2):
                    pe.wait_ge(s["h2_input"], 2 * t + j + 1)
                    transposes(f"h2T{t}{j}", [h2[:, t, (4 * j + k) * P:(4 * j + k + 1) * P] for k in range(4)])

            u0 = FIRST_UNIT["fg0"]
            units(u0 - 5)
            for u in range(u0 - 4, u0):
                products(u, 0)
            for u in range(u0 - 4, u0 - 1):
                products(u, 1)
            second_input(0)
            products(u0 - 1, 1)
            after_job(pe, "h2T01")
            for u in range(u0, u0 + 3):
                products(u, 0)
            second_input(1)
            products(u0 + 3, 0)
            after_job(pe, "h2T11")
            for u in range(u0, u0 + 4):
                products(u, 1)
            next_unit[0] = u0 + 4
            for j in range(5):
                if j:
                    units(LAST_UNIT[f"fu{j - 1}"] + 2)
                    after_block(pe, f"fu{j - 1}")
                    for i in range(2):
                        transposes(f"fT{2 * (j - 1) + i}", tiles(fa[:, (j - 1) % 2], 2 * i))
                units(LAST_UNIT[f"fu{j}"])
            units(LAST_UNIT["fu4"] + 2)
            after_block(pe, "fu4")
            for i in range(2):
                transposes(f"fT{8 + i}", tiles(fa[:, 0], 2 * i))
            units(LAST_UNIT["fgu"])
            after_job(pe, "fT9")
            units(LAST_UNIT["fgu"] + 3)
            after_block(pe, "fgu")
            transposes("fT10", tiles(fa[:, 1], 0))
            units(LAST_UNIT["down0"] - 1)
            after_job(pe, "fT10")
            units(LAST_UNIT["down1"] - SPLIT)
            units_by_tile(LAST_UNIT["down1"])


def weight_stream(w_in, w_uk, w_uv, w_branch, w_out, w_ffn_in, w_ffn_out):
    start = {n: c for n, c, _ in IN_BLOCKS}
    parts = []
    for b, kt, w in UNITS:
        name = BLOCKS[b][0]
        if name in start:
            pieces = [(w_in, start[name], w)]
        elif name.startswith("gate"):
            pieces = [(w_in, C_G + int(name[4]) * D + int(name[5]) * 512, 512)]
        elif name.startswith("branch"):
            pieces = [(w_branch[int(name[6])], int(name[7]) * 512, 512)]
        elif name.startswith("out"):
            pieces = [(w_out, int(name[3]) * 512, 512)]
        elif name in ("uk", "uv"):
            pieces = [(w_uk if name == "uk" else w_uv, 0, HW)]
        elif name == "fgu":
            pieces = [(w_ffn_in, 5 * 512, 256), (w_ffn_in, DFF + 5 * 512, 256)]
        elif name.startswith("fg"):
            pieces = [(w_ffn_in, int(name[2]) * 512, 512)]
        elif name.startswith("fu"):
            pieces = [(w_ffn_in, DFF + int(name[2]) * 512, 512)]
        else:
            pieces = [(w_ffn_out, int(name[4]) * 512, 512)]
        rows = slice(kt * P, (kt + 2) * P)
        unit = np.concatenate([m[rows, c:c + n] for m, c, n in pieces], axis=1)
        parts.append(unit.reshape(2, P, w).transpose(1, 0, 2).reshape(-1))
    return np.concatenate(parts)


def kernel(x, w_in, pre_mix_norm, post_mix_norm, pre_ffn_norm, post_ffn_norm, hg_lb_logits, hg_norm_w, dsa_kv_norm,
           dsa_w_uk, dsa_w_uv, idx_k_norm_w, idx_k_norm_b, rel_bias, w_branch_a, w_branch_b, w_branch_c, w_out,
           w_ffn_in, w_ffn_out):
    import concourse.bacc as bacc
    from concourse.bass_utils import run_bass_kernel_spmd

    w_in, w_out, w_ffn_in, w_ffn_out = (np.asarray(a)[0] for a in (w_in, w_out, w_ffn_in, w_ffn_out))
    w_branch = [np.asarray(a)[0] for a in (w_branch_a, w_branch_b, w_branch_c)]

    def by_partition(a):
        return np.asarray(a).reshape(-1, P).T

    def twice(a):
        return np.concatenate([np.asarray(a).reshape(DI, 1)] * 2)

    eye, levels, hot = constants()
    arrays = {
        "w_stream": weight_stream(w_in, np.asarray(dsa_w_uk).reshape(RK, HW), np.asarray(dsa_w_uv).reshape(RK, HW), w_branch, w_out, w_ffn_in, w_ffn_out),
        "x_in": np.ascontiguousarray(x),
        "cols_in": np.ascontiguousarray(np.concatenate(
            [by_partition(pre_mix_norm), by_partition(hg_lb_logits), by_partition(dsa_kv_norm),
             twice(idx_k_norm_w), twice(idx_k_norm_b)], axis=1)),
        "eye_in": eye, "levels_in": levels, "hot_in": hot,
        "rel_in": np.ascontiguousarray(np.concatenate([np.asarray(rel_bias)], axis=1)),
        "hg_norm": np.ascontiguousarray(hg_norm_w),
        "post_mix": np.ascontiguousarray(post_mix_norm),
        "pre_ffn": np.ascontiguousarray(pre_ffn_norm),
        "post_ffn": np.ascontiguousarray(post_ffn_norm),
    }
    nc = bacc.Bacc("TRN2", target_bir_lowering=False, num_devices=1, dynamic_dma_scratch_size=1024)
    args = {n: nc.dram_tensor(n, a.shape, mybir.dt.from_np(a.dtype), kind="ExternalInput").ap() for n, a in arrays.items()}
    out = nc.dram_tensor("out", (1, S, D), F32, kind="ExternalOutput").ap()
    build_block(nc, **args, out=out)
    r = run_bass_kernel_spmd(nc, [arrays], core_ids=[0])
    return r.results[0]["out"]
```
